# Optimizing a Trainium2 kernel written in Bass

```python
import math
import jax, jax.numpy as jnp
from jax import lax
import numpy as np
import jax
import jax.numpy as jnp

D_MODEL = 1024
BATCH = 1
SEQ = 256
DEPTH = 2

REL_BUCKETS = 32
REL_MAX_EXACT = 16
REL_MAX_DIST = 128
ATTN_HEADS = 8

GLA_HEADS = 4
GLA_DK = 64
GLA_DV = 128
GLA_RANK = 16
GLA_TAU = 16.0
GLA_CHUNK = 64

SWA_HEADS = ATTN_HEADS
SWA_KV_HEADS = 2
SWA_DH = 64
SWA_WINDOW = 128

MOBA_HEADS = ATTN_HEADS
MOBA_KV_HEADS = 2
MOBA_DH = 128
MOBA_BLOCK = 256
MOBA_TOPK = 3
MOBA_Q_CHUNK = 32

EPS = 1e-6

A_WIDTH = GLA_HEADS * GLA_DV
B_WIDTH = SWA_HEADS * SWA_DH
C_WIDTH = MOBA_HEADS * MOBA_DH
EVEN_WIDTH = A_WIDTH + B_WIDTH
EVEN_SPLITS = (GLA_HEADS * GLA_DK, GLA_HEADS * GLA_DK, A_WIDTH, GLA_RANK, A_WIDTH,
               B_WIDTH, SWA_KV_HEADS * SWA_DH, SWA_KV_HEADS * SWA_DH, B_WIDTH)
EVEN_COLS = 2832
ODD_SPLITS = (C_WIDTH, MOBA_KV_HEADS * MOBA_DH, MOBA_KV_HEADS * MOBA_DH, C_WIDTH)
ODD_COLS = 2560
N_EVEN = (DEPTH + 1) // 2
N_ODD = DEPTH // 2


def rmsnorm(x, g):
    xf = x.astype(jnp.float32)
    y = xf * lax.rsqrt(jnp.mean(xf * xf, axis=-1, keepdims=True) + EPS)
    return (y * g.astype(jnp.float32)).astype(x.dtype)

def split_cols(h, sizes):
    idx = np.cumsum(np.array(sizes))[:-1].tolist()
    return jnp.split(h, idx, axis=-1)

def t5_bucket(dist):
    n = jnp.maximum(dist, 0)
    nf = jnp.maximum(n, 1).astype(jnp.float32)
    large = REL_MAX_EXACT + (jnp.log(nf / REL_MAX_EXACT) / math.log(REL_MAX_DIST / REL_MAX_EXACT)
                             * (REL_BUCKETS - REL_MAX_EXACT)).astype(jnp.int32)
    large = jnp.minimum(large, REL_BUCKETS - 1)
    return jnp.where(n < REL_MAX_EXACT, n, large)

def gla_chunked(q, k, v, log_a):
    B_, S_, H_, DK = q.shape
    DV = v.shape[-1]
    N = S_ // GLA_CHUNK

    def chunks(t):
        return t.astype(jnp.float32).reshape(B_, N, GLA_CHUNK, H_, t.shape[-1]).transpose(0, 3, 1, 2, 4)

    qc, kc, vc, gc = chunks(q), chunks(k), chunks(v), chunks(log_a)
    b = jnp.cumsum(gc, axis=3)
    b_last = b[:, :, :, -1:, :]
    q_e = qc * jnp.exp(b) * (DK ** -0.5)
    k_e = kc * jnp.exp(-b)
    causal = jnp.tril(jnp.ones((GLA_CHUNK, GLA_CHUNK), dtype=bool))
    att = jnp.where(causal, jnp.einsum('bhncd,bhnsd->bhncs', q_e, k_e), 0.0)
    o_intra = jnp.einsum('bhncs,bhnse->bhnce', att, vc)
    kv_chunk = jnp.einsum('bhncd,bhnce->bhnde', kc * jnp.exp(b_last - b), vc)
    decay = jnp.exp(b_last[:, :, :, 0, :])

    def step(state, inp):
        dec, kv = inp
        return dec[..., None] * state + kv, state

    s0 = jnp.zeros((B_, H_, DK, DV), jnp.float32)
    _, s_before = lax.scan(step, s0, (jnp.moveaxis(decay, 2, 0), jnp.moveaxis(kv_chunk, 2, 0)))
    s_before = jnp.moveaxis(s_before, 0, 2)
    o = o_intra + jnp.einsum('bhncd,bhnde->bhnce', q_e, s_before)
    return o.transpose(0, 2, 3, 1, 4).reshape(B_, S_, H_, DV).astype(v.dtype)

def swa_attention(q, k, v, sinks, rel_bias):
    B_, S_, H_, DH = q.shape
    KVH = k.shape[2]
    G = H_ // KVH
    W = SWA_WINDOW
    NB = S_ // W
    qb = q.reshape(B_, NB, W, KVH, G, DH).transpose(0, 3, 4, 1, 2, 5)

    def band(t):
        tb = t.reshape(B_, NB, W, KVH, DH).transpose(0, 3, 1, 2, 4)
        prev = jnp.pad(tb[:, :, :-1], ((0, 0), (0, 0), (1, 0), (0, 0), (0, 0)))
        return jnp.concatenate([prev, tb], axis=3)

    kb, vb = band(k), band(v)
    qi = jnp.arange(W)[:, None]
    kj = jnp.arange(2 * W)[None, :]
    dist = qi + W - kj
    in_win = (dist >= 0) & (dist < W)
    blk = jnp.arange(NB)[:, None, None]
    mask = in_win[None] & ((blk > 0) | (kj[None] >= W))
    bias = rel_bias[t5_bucket(dist)].astype(jnp.float32)
    bias = bias.transpose(2, 0, 1).reshape(KVH, G, 1, W, 2 * W)
    logits = jnp.einsum('bkgnqd,bknsd->bkgnqs', qb, kb).astype(jnp.float32) * (DH ** -0.5) + bias
    logits = jnp.where(mask, logits, -jnp.inf)
    sink = jnp.broadcast_to(sinks.astype(jnp.float32).reshape(KVH, G, 1, 1, 1), logits.shape[:-1] + (1,))
    probs = jax.nn.softmax(jnp.concatenate([logits, sink], axis=-1), axis=-1)[..., :-1]
    o = jnp.einsum('bkgnqs,bknsd->bkgnqd', probs.astype(v.dtype), vb)
    return o.transpose(0, 3, 4, 1, 2, 5).reshape(B_, S_, H_ * DH)

def moba_attention(q, k, v, rel_bias):
    B_, S_, H_, DH = q.shape
    G = H_ // k.shape[2]
    S_pad = -(-S_ // MOBA_BLOCK) * MOBA_BLOCK
    pad = ((0, 0), (0, S_pad - S_), (0, 0), (0, 0))
    qh = jnp.pad(q, pad).transpose(0, 2, 1, 3)
    kh = jnp.repeat(jnp.pad(k, pad), G, axis=2).transpose(0, 2, 1, 3)
    vh = jnp.repeat(jnp.pad(v, pad), G, axis=2).transpose(0, 2, 1, 3)
    NBLK = S_pad // MOBA_BLOCK
    kblk = kh.reshape(B_, H_, NBLK, MOBA_BLOCK, DH)
    vblk = vh.reshape(B_, H_, NBLK, MOBA_BLOCK, DH)
    kmean = kblk.mean(axis=3)
    k_sel = min(MOBA_TOPK, NBLK)
    bi = jnp.arange(B_)[:, None, None, None]
    hi = jnp.arange(H_)[None, :, None, None]
    offs = jnp.arange(MOBA_BLOCK)
    blk_ids = jnp.arange(NBLK)
    scale = DH ** -0.5

    def one_chunk(c):
        start = c * MOBA_Q_CHUNK
        qc = lax.dynamic_slice_in_dim(qh, start, MOBA_Q_CHUNK, axis=2)
        tpos = start + jnp.arange(MOBA_Q_CHUNK)
        own = start // MOBA_BLOCK
        gate = jnp.einsum('bhqd,bhnd->bhqn', qc, kmean).astype(jnp.float32)
        gate = jnp.where(blk_ids < own, gate, -jnp.inf)
        _, idx = lax.top_k(gate, k_sel)
        kg = kblk[bi, hi, idx].reshape(B_, H_, MOBA_Q_CHUNK, k_sel * MOBA_BLOCK, DH)
        vg = vblk[bi, hi, idx].reshape(B_, H_, MOBA_Q_CHUNK, k_sel * MOBA_BLOCK, DH)
        kpos = (idx[..., None] * MOBA_BLOCK + offs).reshape(B_, H_, MOBA_Q_CHUNK, k_sel * MOBA_BLOCK)
        valid = jnp.broadcast_to((idx < own)[..., None], idx.shape + (MOBA_BLOCK,)).reshape(kpos.shape)
        bias_sel = rel_bias[t5_bucket(tpos[None, None, :, None] - kpos), hi].astype(jnp.float32)
        logit_sel = jnp.einsum('bhqd,bhqsd->bhqs', qc, kg).astype(jnp.float32) * scale + bias_sel
        logit_sel = jnp.where(valid, logit_sel, -jnp.inf)
        ko = lax.dynamic_slice_in_dim(kh, own * MOBA_BLOCK, MOBA_BLOCK, axis=2)
        vo = lax.dynamic_slice_in_dim(vh, own * MOBA_BLOCK, MOBA_BLOCK, axis=2)
        dist_own = tpos[:, None] - (own * MOBA_BLOCK + offs)[None, :]
        bias_own = rel_bias[t5_bucket(dist_own)].astype(jnp.float32).transpose(2, 0, 1)
        logit_own = jnp.einsum('bhqd,bhsd->bhqs', qc, ko).astype(jnp.float32) * scale + bias_own
        logit_own = jnp.where(dist_own >= 0, logit_own, -jnp.inf)
        probs = jax.nn.softmax(jnp.concatenate([logit_sel, logit_own], axis=-1), axis=-1)
        p_sel = probs[..., :k_sel * MOBA_BLOCK]
        p_own = probs[..., k_sel * MOBA_BLOCK:]
        o = jnp.einsum('bhqs,bhqsd->bhqd', p_sel, vg) + jnp.einsum('bhqs,bhsd->bhqd', p_own, vo)
        return o.astype(v.dtype)

    out = lax.map(one_chunk, jnp.arange(S_pad // MOBA_Q_CHUNK))
    out = out.transpose(1, 0, 3, 2, 4).reshape(B_, S_pad, H_ * DH)
    return out[:, :S_]

def even_layer(hn, w_in, gla_w_up, gla_b_up, gla_gain, sinks, w_out, rel_bias):
    B_, S_, _ = hn.shape
    proj = hn @ w_in
    aq, ak, av, a_down, a_gate, bq, bk, bv, b_gate = split_cols(proj, EVEN_SPLITS)
    log_a = jax.nn.log_sigmoid((a_down @ gla_w_up + gla_b_up).astype(jnp.float32)) / GLA_TAU
    oa = gla_chunked(aq.reshape(B_, S_, GLA_HEADS, GLA_DK), ak.reshape(B_, S_, GLA_HEADS, GLA_DK),
                     av.reshape(B_, S_, GLA_HEADS, GLA_DV), log_a.reshape(B_, S_, GLA_HEADS, GLA_DK))
    oa = rmsnorm(oa, gla_gain).reshape(B_, S_, A_WIDTH) * jax.nn.silu(a_gate)
    ob = swa_attention(bq.reshape(B_, S_, SWA_HEADS, SWA_DH), bk.reshape(B_, S_, SWA_KV_HEADS, SWA_DH),
                       bv.reshape(B_, S_, SWA_KV_HEADS, SWA_DH), sinks, rel_bias) * jax.nn.silu(b_gate)
    return jnp.concatenate([oa, ob], axis=-1) @ w_out

def odd_layer(hn, w_in, w_out, rel_bias):
    B_, S_, _ = hn.shape
    cq, ck, cv, c_gate = split_cols(hn @ w_in, ODD_SPLITS)
    oc = moba_attention(cq.reshape(B_, S_, MOBA_HEADS, MOBA_DH), ck.reshape(B_, S_, MOBA_KV_HEADS, MOBA_DH),
                        cv.reshape(B_, S_, MOBA_KV_HEADS, MOBA_DH), rel_bias)
    return (oc * jax.nn.silu(c_gate)) @ w_out

def first_inputs(seed: int = 0) -> dict:
    key = jax.random.key(seed)
    ks = jax.random.split(key, 12)
    f32 = jnp.float32
    x = jax.random.normal(ks[0], (BATCH, SEQ, D_MODEL), f32)
    norm_gain = 1.0 + 0.02 * jax.random.normal(ks[1], (DEPTH, D_MODEL), f32)
    final_gain = 1.0 + 0.02 * jax.random.normal(ks[2], (D_MODEL,), f32)
    rel_bias = 0.2 * jax.random.normal(ks[3], (REL_BUCKETS, ATTN_HEADS), f32)
    w_in_even = jax.random.normal(ks[4], (N_EVEN, D_MODEL, EVEN_COLS), f32) * D_MODEL ** -0.5
    gla_w_up = jax.random.normal(ks[5], (N_EVEN, GLA_RANK, GLA_HEADS * GLA_DK), f32) * GLA_RANK ** -0.5
    gla_b_up = 0.1 * jax.random.normal(ks[6], (N_EVEN, GLA_HEADS * GLA_DK), f32)
    gla_norm_gain = 1.0 + 0.02 * jax.random.normal(ks[7], (N_EVEN, GLA_DV), f32)
    swa_sinks = 0.5 * jax.random.normal(ks[8], (N_EVEN, SWA_HEADS), f32)
    w_out_even = jax.random.normal(ks[9], (N_EVEN, EVEN_WIDTH, D_MODEL), f32) * EVEN_WIDTH ** -0.5
    w_in_odd = jax.random.normal(ks[10], (N_ODD, D_MODEL, ODD_COLS), f32) * D_MODEL ** -0.5
    w_out_odd = jax.random.normal(ks[11], (N_ODD, C_WIDTH, D_MODEL), f32) * C_WIDTH ** -0.5
    return {"x": x, "norm_gain": norm_gain, "final_gain": final_gain, "rel_bias": rel_bias,
            "w_in_even": w_in_even, "gla_w_up": gla_w_up, "gla_b_up": gla_b_up,
            "gla_norm_gain": gla_norm_gain, "swa_sinks": swa_sinks, "w_out_even": w_out_even,
            "w_in_odd": w_in_odd, "w_out_odd": w_out_odd}

def first_block(x, norm_gain, final_gain, rel_bias, w_in_even, gla_w_up, gla_b_up, gla_norm_gain,
              swa_sinks, w_out_even, w_in_odd, w_out_odd):
    h = x
    for layer in range(DEPTH):
        hn = rmsnorm(h, norm_gain[layer])
        if layer % 2 == 0:
            i = layer // 2
            h = h + even_layer(hn, w_in_even[i], gla_w_up[i], gla_b_up[i], gla_norm_gain[i],
                               swa_sinks[i], w_out_even[i], rel_bias)
        else:
            i = layer // 2
            h = h + odd_layer(hn, w_in_odd[i], w_out_odd[i], rel_bias)
    return rmsnorm(h, final_gain)


PLE_DIM = 256
N_EVEN_2 = (DEPTH + 1) // 2
N_ODD_2 = DEPTH // 2

DA_HEADS = 4
DA_HEAD_DIM = 64
DA_V_DIM = 2 * DA_HEAD_DIM
DA_QK_WIDTH = DA_HEADS * 2 * DA_HEAD_DIM
DA_WIDTH = DA_HEADS * DA_V_DIM
ROPE_THETA = 500000.0
ROT_DIM = DA_HEAD_DIM // 4
Q_BLOCK = 128

SC_WIDTH = 512
SC_WIDTH_CONV = 3
EVEN_IN_WIDTH = 3 * DA_QK_WIDTH // 2 * 2 // 2 * 0 + DA_QK_WIDTH * 2 + DA_WIDTH + 3 * SC_WIDTH

GM_WIDTH = D_MODEL
GM_GROUPS = 8
GM_GROUP_CH = GM_WIDTH // GM_GROUPS
GM_CHUNK = 128

D_FF = 2816
N_EXPERTS = 8
TOP_K = 2
MOE_BLOCK = 256

RMS_EPS = 1e-6
LN_EPS = 1e-5


def rms_norm(x, g):
    xf = x.astype(jnp.float32)
    y = xf * lax.rsqrt(jnp.mean(xf * xf, axis=-1, keepdims=True) + RMS_EPS)
    return (y * g.astype(jnp.float32)).astype(x.dtype)

def layer_norm(x, g, b):
    xf = x.astype(jnp.float32)
    mu = jnp.mean(xf, axis=-1, keepdims=True)
    var = jnp.mean(jnp.square(xf - mu), axis=-1, keepdims=True)
    y = (xf - mu) * lax.rsqrt(var + LN_EPS)
    return (y * g.astype(jnp.float32) + b.astype(jnp.float32)).astype(x.dtype)

def rope_partial(t, positions):
    half = ROT_DIM // 2
    inv_freq = ROPE_THETA ** (-jnp.arange(0, ROT_DIM, 2, dtype=jnp.float32) / ROT_DIM)
    ang = positions.astype(jnp.float32)[:, :, None] * inv_freq
    cos = jnp.cos(ang)[:, :, None, None, :].astype(t.dtype)
    sin = jnp.sin(ang)[:, :, None, None, :].astype(t.dtype)
    t1 = t[..., :half]
    t2 = t[..., half:ROT_DIM]
    return jnp.concatenate([t1 * cos - t2 * sin, t2 * cos + t1 * sin, t[..., ROT_DIM:]], axis=-1)

def diff_attention(q, k, v, lam, lambda_init, subln_g):
    bsz, seq = q.shape[0], q.shape[1]
    n_blocks = seq // Q_BLOCK
    q = q * (DA_HEAD_DIM ** -0.5)
    kpos = jnp.arange(seq)

    def one_block(i):
        qb = lax.dynamic_slice_in_dim(q, i * Q_BLOCK, Q_BLOCK, axis=1)
        s = jnp.einsum('bqhcd,bkhcd->bhcqk', qb, k, preferred_element_type=jnp.float32)
        qpos = i * Q_BLOCK + jnp.arange(Q_BLOCK)
        mask = kpos[None, :] <= qpos[:, None]
        pr = jax.nn.softmax(jnp.where(mask, s, -jnp.inf), axis=-1)
        w = pr[:, :, 0] - lam * pr[:, :, 1]
        return jnp.einsum('bhqk,bkhe->bqhe', w.astype(v.dtype), v)

    out = lax.map(one_block, jnp.arange(n_blocks))
    out = jnp.moveaxis(out, 0, 1).reshape(bsz, seq, DA_HEADS, DA_V_DIM)
    out = rms_norm(out, subln_g) * (1.0 - lambda_init)
    return out.reshape(bsz, seq, DA_WIDTH)

def causal_short_conv(z, w):
    ch = z.shape[-1]
    rhs = jnp.transpose(w).astype(z.dtype)[:, None, :]
    return lax.conv_general_dilated(z, rhs, window_strides=(1,), padding=[(SC_WIDTH_CONV - 1, 0)],
                                    dimension_numbers=('NWC', 'WIO', 'NWC'), feature_group_count=ch)

def spatial_gating(u, v, w_s, b_s):
    bsz, seq, _ = v.shape
    vr = v.reshape(bsz, seq // GM_CHUNK, GM_CHUNK, GM_GROUPS, GM_GROUP_CH)
    tril = jnp.tril(jnp.ones((GM_CHUNK, GM_CHUNK), dtype=w_s.dtype))
    vs = jnp.einsum('gts,bnsgc->bntgc', w_s * tril, vr)
    vs = vs + jnp.transpose(b_s)[None, None, :, :, None]
    return u * vs.reshape(bsz, seq, GM_WIDTH)

def swiglu(h, w1, w3, w2):
    return (jax.nn.silu(h @ w1) * (h @ w3)) @ w2

def moe_swiglu(h, router_w, w1, w3, w2):
    bsz, seq, dm = h.shape
    n_tok = bsz * seq
    n_assign = n_tok * TOP_K
    n_blocks = -(-(n_assign + N_EXPERTS * (MOE_BLOCK - 1)) // MOE_BLOCK)
    xt = h.reshape(n_tok, dm)
    logits = jnp.einsum('nd,de->ne', xt, router_w, preferred_element_type=jnp.float32)
    top_val, top_idx = lax.top_k(logits, TOP_K)
    gates = jax.nn.softmax(top_val, axis=-1)
    expert_flat = top_idx.reshape(-1)
    token_flat = jnp.arange(n_assign) // TOP_K
    gate_flat = gates.reshape(-1)
    order = jnp.argsort(expert_flat)
    sorted_expert = expert_flat[order]
    sorted_token = token_flat[order]
    counts = jnp.bincount(expert_flat, length=N_EXPERTS)
    starts = jnp.cumsum(counts) - counts
    padded = (counts + MOE_BLOCK - 1) // MOE_BLOCK * MOE_BLOCK
    pad_ends = jnp.cumsum(padded)
    pad_starts = pad_ends - padded
    dest = pad_starts[sorted_expert] + (jnp.arange(n_assign) - starts[sorted_expert])
    rows = jnp.zeros((n_blocks * MOE_BLOCK, dm), h.dtype).at[dest].set(xt[sorted_token])
    block_start = jnp.arange(n_blocks) * MOE_BLOCK
    block_expert = jnp.minimum(jnp.searchsorted(pad_ends, block_start, side='right'), N_EXPERTS - 1)

    def expert_block(args):
        xb, e = args
        return (jax.nn.silu(xb @ w1[e]) * (xb @ w3[e])) @ w2[e]

    y_rows = lax.map(expert_block, (rows.reshape(n_blocks, MOE_BLOCK, dm), block_expert))
    y_sorted = y_rows.reshape(n_blocks * MOE_BLOCK, dm)[dest]
    contrib = y_sorted * gate_flat[order][:, None].astype(h.dtype)
    out = jax.ops.segment_sum(contrib, sorted_token, num_segments=n_tok)
    return out.reshape(bsz, seq, dm)

def second_inputs(seed: int = 0) -> dict:
    key = jax.random.key(seed)
    ks = list(jax.random.split(key, 40))
    cnt = [0]

    def nk():
        cnt[0] += 1
        return ks[cnt[0] - 1]

    def nrm(shape, scale):
        return scale * jax.random.normal(nk(), shape, jnp.float32)

    def gain(shape):
        return 1.0 + nrm(shape, 0.05)

    x = nrm((BATCH, SEQ, D_MODEL), 1.0)
    p = nrm((DEPTH, BATCH, SEQ, PLE_DIM), 1.0)
    positions = (jax.random.randint(nk(), (BATCH, 1), 0, 1024, jnp.int32)
                 + jnp.arange(SEQ, dtype=jnp.int32)[None, :])
    dsc = D_MODEL ** -0.5
    return {
        "x": x,
        "p": p,
        "positions": positions,
        "ln_mix": gain((DEPTH, D_MODEL)),
        "ln_ffn": gain((DEPTH, D_MODEL)),
        "ln_ple": gain((DEPTH, D_MODEL)),
        "a_w_in": nrm((N_EVEN_2, D_MODEL, EVEN_IN_WIDTH), dsc),
        "a_lambda": nrm((N_EVEN_2, 4, DA_HEAD_DIM), 0.1),
        "a_subln": gain((N_EVEN_2, DA_V_DIM)),
        "a_conv_w": nrm((N_EVEN_2, SC_WIDTH, SC_WIDTH_CONV), SC_WIDTH_CONV ** -0.5),
        "a_w_out": nrm((N_EVEN_2, DA_WIDTH + SC_WIDTH, D_MODEL), (DA_WIDTH + SC_WIDTH) ** -0.5),
        "ffn_w1": nrm((N_EVEN_2, D_MODEL, D_FF), dsc),
        "ffn_w3": nrm((N_EVEN_2, D_MODEL, D_FF), dsc),
        "ffn_w2": nrm((N_EVEN_2, D_FF, D_MODEL), D_FF ** -0.5),
        "c_w_in": nrm((N_ODD_2, D_MODEL, 2 * GM_WIDTH), dsc),
        "c_ln_g": gain((N_ODD_2, GM_WIDTH)),
        "c_ln_b": nrm((N_ODD_2, GM_WIDTH), 0.02),
        "c_w_s": nrm((N_ODD_2, GM_GROUPS, GM_CHUNK, GM_CHUNK), GM_CHUNK ** -0.5),
        "c_b_s": 1.0 + nrm((N_ODD_2, GM_GROUPS, GM_CHUNK), 0.1),
        "c_w_out": nrm((N_ODD_2, GM_WIDTH, D_MODEL), GM_WIDTH ** -0.5),
        "router_w": nrm((N_ODD_2, D_MODEL, N_EXPERTS), dsc),
        "moe_w1": nrm((N_ODD_2, N_EXPERTS, D_MODEL, D_FF), dsc),
        "moe_w3": nrm((N_ODD_2, N_EXPERTS, D_MODEL, D_FF), dsc),
        "moe_w2": nrm((N_ODD_2, N_EXPERTS, D_FF, D_MODEL), D_FF ** -0.5),
        "ple_gate": nrm((DEPTH, D_MODEL, D_MODEL), dsc),
        "ple_proj": nrm((DEPTH, PLE_DIM, D_MODEL), PLE_DIM ** -0.5),
        "final_norm": gain((D_MODEL,)),
    }

def second_block(x, p, positions, ln_mix, ln_ffn, ln_ple, a_w_in, a_lambda, a_subln, a_conv_w,
              a_w_out, ffn_w1, ffn_w3, ffn_w2, c_w_in, c_ln_g, c_ln_b, c_w_s, c_b_s, c_w_out,
              router_w, moe_w1, moe_w3, moe_w2, ple_gate, ple_proj, final_norm):
    h = x
    bsz, seq, _ = x.shape
    splits = [DA_QK_WIDTH, 2 * DA_QK_WIDTH, 2 * DA_QK_WIDTH + DA_WIDTH,
              2 * DA_QK_WIDTH + DA_WIDTH + SC_WIDTH, 2 * DA_QK_WIDTH + DA_WIDTH + 2 * SC_WIDTH]
    for i in range(DEPTH):
        j = i // 2
        hn = rms_norm(h, ln_mix[i])
        if i % 2 == 0:
            z = hn @ a_w_in[j]
            q, k, v, b_gate, c_gate, hc = jnp.split(z, splits, axis=-1)
            q = rope_partial(q.reshape(bsz, seq, DA_HEADS, 2, DA_HEAD_DIM), positions)
            k = rope_partial(k.reshape(bsz, seq, DA_HEADS, 2, DA_HEAD_DIM), positions)
            v = v.reshape(bsz, seq, DA_HEADS, DA_V_DIM)
            lambda_init = 0.8 - 0.6 * math.exp(-0.3 * i)
            lp = a_lambda[j].astype(jnp.float32)
            lam = jnp.exp(jnp.sum(lp[0] * lp[1])) - jnp.exp(jnp.sum(lp[2] * lp[3])) + lambda_init
            attn = diff_attention(q, k, v, lam, lambda_init, a_subln[j])
            conv = b_gate * causal_short_conv(c_gate * hc, a_conv_w[j])
            h = h + jnp.concatenate([attn, conv], axis=-1) @ a_w_out[j]
            h = h + swiglu(rms_norm(h, ln_ffn[i]), ffn_w1[j], ffn_w3[j], ffn_w2[j])
        else:
            z = jax.nn.gelu(hn @ c_w_in[j], approximate=False)
            u, vv = jnp.split(z, 2, axis=-1)
            vv = layer_norm(vv, c_ln_g[j], c_ln_b[j])
            h = h + spatial_gating(u, vv, c_w_s[j], c_b_s[j]) @ c_w_out[j]
            h = h + moe_swiglu(rms_norm(h, ln_ffn[i]), router_w[j], moe_w1[j], moe_w3[j], moe_w2[j])
        gate = jax.nn.sigmoid(rms_norm(h, ln_ple[i]) @ ple_gate[i])
        h = h + gate * (p[i] @ ple_proj[i])
    return rms_norm(h, final_norm)


DEPTH_3 = 1

N_META = 16
ROPE_THETA_3 = 10000.0
BLOCK_Q = 128
MLA_HEADS = 8
MLA_Q_RANK = 256
MLA_KV_RANK = 128
MLA_NOPE_DIM = 64
MLA_ROPE_DIM = 32
MLA_QK_DIM = MLA_NOPE_DIM + MLA_ROPE_DIM
MLA_V_DIM = 64
DSA_HEADS = 8
DSA_HEAD_DIM = 64
IDX_HEADS = 8
IDX_DIM = 64
TOPK_MAX = 256
MIX_WIDTH = MLA_HEADS * MLA_V_DIM + DSA_HEADS * DSA_HEAD_DIM
IN_SIZES = (MLA_Q_RANK, MLA_KV_RANK, MLA_ROPE_DIM,
            DSA_HEADS * DSA_HEAD_DIM, DSA_HEADS * DSA_HEAD_DIM, DSA_HEADS * DSA_HEAD_DIM,
            IDX_HEADS * IDX_DIM, IDX_DIM, IDX_HEADS)
C_IN = sum(IN_SIZES)
D_FF_RAW = -(-8 * D_MODEL // 3)
D_FF_3 = -(-D_FF_RAW // 256) * 256


def rmsnorm_3(x, g):
    x32 = x.astype(jnp.float32)
    y = x32 * lax.rsqrt(jnp.mean(x32 * x32, axis=-1, keepdims=True) + EPS)
    return (y * g.astype(jnp.float32)).astype(x.dtype)

def rope(x, pos):
    half = x.shape[-1] // 2
    inv = jnp.power(ROPE_THETA_3, -jnp.arange(half, dtype=jnp.float32) / half)
    ang = pos.astype(jnp.float32)[:, None] * inv[None, :]
    cos = jnp.cos(ang)[:, None, :]
    sin = jnp.sin(ang)[:, None, :]
    x32 = x.astype(jnp.float32)
    x1, x2 = x32[..., :half], x32[..., half:]
    return jnp.concatenate([x1 * cos - x2 * sin, x2 * cos + x1 * sin], axis=-1).astype(x.dtype)

def to_blocks(a):
    b, tp = a.shape[0], a.shape[1]
    return a.reshape((b, tp // BLOCK_Q, BLOCK_Q) + a.shape[2:]).swapaxes(0, 1)

def from_blocks(a):
    a = a.swapaxes(0, 1)
    return a.reshape((a.shape[0], a.shape[1] * a.shape[2]) + a.shape[3:])

def causal_block_attention(q, k, v):
    tp = q.shape[1]
    scale = q.shape[-1] ** -0.5
    kpos = jnp.arange(tp)

    def one_block(args):
        qb, blk = args
        qpos = blk * BLOCK_Q + jnp.arange(BLOCK_Q)
        s = jnp.einsum('bqhd,bkhd->bhqk', qb, k, preferred_element_type=jnp.float32) * scale
        s = jnp.where((kpos[None, :] <= qpos[:, None])[None, None], s, -jnp.inf)
        p = jax.nn.softmax(s, axis=-1).astype(v.dtype)
        return jnp.einsum('bhqk,bkhd->bqhd', p, v)

    out = lax.map(one_block, (to_blocks(q), jnp.arange(tp // BLOCK_Q)))
    return from_blocks(out)

def indexed_sparse_attention(q, k, v, q_idx, k_idx, w_idx, topk):
    tp = q.shape[1]
    scale = q.shape[-1] ** -0.5
    idx_scale = IDX_DIM ** -0.5
    kpos = jnp.arange(tp)

    def one_block(args):
        qb, qib, wib, blk = args
        qpos = blk * BLOCK_Q + jnp.arange(BLOCK_Q)
        causal = kpos[None, :] <= qpos[:, None]
        logits = jnp.einsum('bqhd,bkd->bqhk', qib, k_idx, preferred_element_type=jnp.float32) * idx_scale
        score = jnp.einsum('bqh,bqhk->bqk', wib.astype(jnp.float32), jax.nn.relu(logits))
        score = jnp.where(causal[None], score, -jnp.inf)
        _, sel = lax.top_k(score, topk)
        valid = sel <= qpos[None, :, None]
        k_sel = jax.vmap(lambda kb, ib: kb[ib])(k, sel)
        v_sel = jax.vmap(lambda vb, ib: vb[ib])(v, sel)
        s = jnp.einsum('bqhd,bqkhd->bhqk', qb, k_sel, preferred_element_type=jnp.float32) * scale
        s = jnp.where(valid[:, None], s, -jnp.inf)
        p = jax.nn.softmax(s, axis=-1).astype(v.dtype)
        return jnp.einsum('bhqk,bqkhd->bqhd', p, v_sel)

    out = lax.map(one_block, (to_blocks(q), to_blocks(q_idx), to_blocks(w_idx), jnp.arange(tp // BLOCK_Q)))
    return from_blocks(out)

def hybrid_mixer(u, pos, topk, w_in, q_norm_g, w_uq, kv_norm_g, w_ukv, w_o):
    b, tp, _ = u.shape
    proj = u @ w_in
    splits = [int(v) for v in np.cumsum(IN_SIZES)[:-1]]
    c_q, c_kv, k_r, q_s, k_s, v_s, q_i, k_i, w_i = jnp.split(proj, splits, axis=-1)

    q = (rmsnorm_3(c_q, q_norm_g) @ w_uq).reshape(b, tp, MLA_HEADS, MLA_QK_DIM)
    q_mla = jnp.concatenate([q[..., :MLA_NOPE_DIM], rope(q[..., MLA_NOPE_DIM:], pos)], axis=-1)
    kv = (rmsnorm_3(c_kv, kv_norm_g) @ w_ukv).reshape(b, tp, MLA_HEADS, MLA_NOPE_DIM + MLA_V_DIM)
    k_rope = rope(k_r[:, :, None, :], pos)
    k_mla = jnp.concatenate([kv[..., :MLA_NOPE_DIM],
                             jnp.broadcast_to(k_rope, (b, tp, MLA_HEADS, MLA_ROPE_DIM))], axis=-1)
    v_mla = kv[..., MLA_NOPE_DIM:]
    o_mla = causal_block_attention(q_mla, k_mla, v_mla)

    q_s = rope(q_s.reshape(b, tp, DSA_HEADS, DSA_HEAD_DIM), pos)
    k_s = rope(k_s.reshape(b, tp, DSA_HEADS, DSA_HEAD_DIM), pos)
    v_s = v_s.reshape(b, tp, DSA_HEADS, DSA_HEAD_DIM)
    q_i = rope(q_i.reshape(b, tp, IDX_HEADS, IDX_DIM), pos)
    k_i = rope(k_i[:, :, None, :], pos)[:, :, 0, :]
    w_i = w_i * (IDX_HEADS ** -0.5)
    o_dsa = indexed_sparse_attention(q_s, k_s, v_s, q_i, k_i, w_i, topk)

    o = jnp.concatenate([o_mla.reshape(b, tp, MLA_HEADS * MLA_V_DIM),
                         o_dsa.reshape(b, tp, DSA_HEADS * DSA_HEAD_DIM)], axis=-1)
    return o @ w_o

def swiglu_3(u, w_gate, w_up, w_down):
    return (jax.nn.silu(u @ w_gate) * (u @ w_up)) @ w_down

def third_inputs(seed: int = 0) -> dict:
    key = jax.random.key(seed)
    ks = jax.random.split(key, 16)
    f32 = jnp.float32

    def w(k, shape, fan_in):
        return jax.random.normal(k, shape, f32) * (fan_in ** -0.5)

    def g(k, shape):
        return 1.0 + 0.02 * jax.random.normal(k, shape, f32)

    return {
        'x': jax.random.normal(ks[0], (BATCH, SEQ, D_MODEL), f32),
        'meta_tokens': jax.random.normal(ks[1], (N_META, D_MODEL), f32),
        'attn_norm_g': g(ks[2], (DEPTH_3, D_MODEL)),
        'w_in': w(ks[3], (DEPTH_3, D_MODEL, C_IN), D_MODEL),
        'mla_q_norm_g': g(ks[4], (DEPTH_3, MLA_Q_RANK)),
        'w_uq': w(ks[5], (DEPTH_3, MLA_Q_RANK, MLA_HEADS * MLA_QK_DIM), MLA_Q_RANK),
        'mla_kv_norm_g': g(ks[6], (DEPTH_3, MLA_KV_RANK)),
        'w_ukv': w(ks[7], (DEPTH_3, MLA_KV_RANK, MLA_HEADS * (MLA_NOPE_DIM + MLA_V_DIM)), MLA_KV_RANK),
        'w_o': w(ks[8], (DEPTH_3, MIX_WIDTH, D_MODEL), MIX_WIDTH),
        'ffn_norm_g': g(ks[9], (DEPTH_3, D_MODEL)),
        'w_gate': w(ks[10], (DEPTH_3, D_MODEL, D_FF_3), D_MODEL),
        'w_up': w(ks[11], (DEPTH_3, D_MODEL, D_FF_3), D_MODEL),
        'w_down': w(ks[12], (DEPTH_3, D_FF_3, D_MODEL), D_FF_3),
        'final_norm_g': g(ks[13], (D_MODEL,)),
    }

def third_block(x, meta_tokens, attn_norm_g, w_in, mla_q_norm_g, w_uq, mla_kv_norm_g, w_ukv, w_o,
              ffn_norm_g, w_gate, w_up, w_down, final_norm_g):
    b, seq, _ = x.shape
    topk = min(TOPK_MAX, seq // 4)
    meta = jnp.broadcast_to(meta_tokens[None].astype(x.dtype), (b, N_META, D_MODEL))
    h = jnp.concatenate([meta, x], axis=1)
    t = h.shape[1]
    tp = -(-t // BLOCK_Q) * BLOCK_Q
    h = jnp.pad(h, ((0, 0), (0, tp - t), (0, 0)))
    pos = jnp.arange(tp, dtype=jnp.int32)
    for l in range(DEPTH_3):
        h = h + hybrid_mixer(rmsnorm_3(h, attn_norm_g[l]), pos, topk, w_in[l], mla_q_norm_g[l], w_uq[l],
                             mla_kv_norm_g[l], w_ukv[l], w_o[l])
        h = h + swiglu_3(rmsnorm_3(h, ffn_norm_g[l]), w_gate[l], w_up[l], w_down[l])
    h = rmsnorm_3(h, final_norm_g)
    return h[:, N_META:t]


def setup_inputs(seed=0):
    out = dict(first_inputs(seed))
    for name, value in second_inputs(seed + 1).items():
        if name != "x":
            out[name + "_2"] = value
    for name, value in third_inputs(seed + 2).items():
        if name != "x":
            out[name + "_3"] = value
    return out


def reference(
    x, norm_gain, final_gain, rel_bias, w_in_even, gla_w_up, gla_b_up, gla_norm_gain, swa_sinks,
    w_out_even, w_in_odd, w_out_odd, p_2, positions_2, ln_mix_2, ln_ffn_2, ln_ple_2, a_w_in_2,
    a_lambda_2, a_subln_2, a_conv_w_2, a_w_out_2, ffn_w1_2, ffn_w3_2, ffn_w2_2, c_w_in_2,
    c_ln_g_2, c_ln_b_2, c_w_s_2, c_b_s_2, c_w_out_2, router_w_2, moe_w1_2, moe_w3_2, moe_w2_2,
    ple_gate_2, ple_proj_2, final_norm_2, meta_tokens_3, attn_norm_g_3, w_in_3, mla_q_norm_g_3,
    w_uq_3, mla_kv_norm_g_3, w_ukv_3, w_o_3, ffn_norm_g_3, w_gate_3, w_up_3, w_down_3,
    final_norm_g_3,
):
    x = first_block(
        x, norm_gain, final_gain, rel_bias, w_in_even, gla_w_up, gla_b_up, gla_norm_gain,
        swa_sinks, w_out_even, w_in_odd, w_out_odd,
    )
    x = second_block(
        x, p_2, positions_2, ln_mix_2, ln_ffn_2, ln_ple_2, a_w_in_2, a_lambda_2, a_subln_2,
        a_conv_w_2, a_w_out_2, ffn_w1_2, ffn_w3_2, ffn_w2_2, c_w_in_2, c_ln_g_2, c_ln_b_2,
        c_w_s_2, c_b_s_2, c_w_out_2, router_w_2, moe_w1_2, moe_w3_2, moe_w2_2, ple_gate_2,
        ple_proj_2, final_norm_2,
    )
    return third_block(
        x, meta_tokens_3, attn_norm_g_3, w_in_3, mla_q_norm_g_3, w_uq_3, mla_kv_norm_g_3,
        w_ukv_3, w_o_3, ffn_norm_g_3, w_gate_3, w_up_3, w_down_3, final_norm_g_3,
    )


_drawn_inputs = setup_inputs


def setup_inputs(seed=0):
    import zlib

    import numpy as np

    out = dict(_drawn_inputs(seed))
    spreads = {}
    factors = {'c_ln_b_2': 2.748,
     'attn_norm_g_3': 2.7,
     'mla_q_norm_g_3': 8.0,
     'mla_kv_norm_g_3': 8.0,
     'ffn_norm_g_3': 4.087,
     'final_norm_g_3': 2.979}
    for name, (base, spread) in spreads.items():
        noise = np.random.default_rng([zlib.crc32(name.encode()), seed]).standard_normal(out[name].shape)
        drawn = base * np.exp(spread * noise) if base else spread * noise
        out[name] = jnp.asarray(drawn.astype(out[name].dtype))
    for name, factor in factors.items():
        out[name] = (out[name] * factor).astype(out[name].dtype)
    return out
```

```python
from contextlib import contextmanager

import concourse.bass as bass
from concourse import mybir

F32 = mybir.dt.float32
I32 = mybir.dt.int32
U32 = mybir.dt.uint32
ALU = mybir.AluOpType
ACT = mybir.ActivationFunctionType
AX_X = mybir.AxisListType.X
ENG = mybir.EngineType
ds = bass.ds

P = 128
D = 1024
KT = D // P
SEQ = 256
NT = SEQ // P
META = 16
KEYS3 = META + SEQ
CHUNK = 2048
CW = CHUNK // KT
RING = 8
LAND = 3
FF = 2816
FG = FF // (2 * P)
NEXP = 8
TOPK3 = 64
NEG = -1.0e30
TAKEN = -3.0e38
PI = 3.141592653589793

N_IN1, N_OUT, N_ODD, N_IN2, N_CIN, N_IN3 = 12, 4, 10, 12, 8, 10
FFN_CHUNKS = 3 * FG

CONSTS = {}
_at = 0
for _name, _width in (("ident", P), ("flip", P), ("tri", P), ("same", P), ("half", 2), ("tril", P),
                      ("causal", NT * SEQ), ("causal3", NT * KEYS3), ("cos16", 48), ("sin16", 48),
                      ("cos32", 96), ("sin32", 96), ("experts", NEXP)):
    CONSTS[_name] = (_at, _width)
    _at += _width
N_CONST = _at

COLS = {}
_at = 0
for _name, _width in (("norm0", 8), ("norm1", 8), ("mix0", 8), ("mix1", 8), ("ffn0", 8), ("ffn1", 8),
                      ("ple0", 8), ("ple1", 8), ("attn3", 8), ("ffn3", 8), ("q3", 2), ("kv3", 1),
                      ("conv", 12), ("bs", 8)):
    COLS[_name] = (_at, _width)
    _at += _width
N_COLS = _at

ROWS = {}
_at = 0
for _name, _width in (("final1", D), ("lng", D), ("lnb", D), ("final2", D), ("final3", D), ("gla", P),
                      ("subln", P), ("sinks", 8), ("lambda", 256), ("freq", 8)):
    ROWS[_name] = (_at, _width)
    _at += _width
N_ROWS = _at


class Lane:

    def __init__(self, name, eng, sem):
        self.name, self.e, self.sem = name, eng, sem
        self.n = 0
        self.turn = 0
        self.seen = {}

    def now(self):
        return (self.sem, self.turn + self.n if self.n else 0)

    def did(self, ins):
        ins.then_inc(self.sem, 1)
        self.n += 1
        return self.now()

    def wait(self, *tokens):
        for token in tokens:
            if token is None:
                continue
            sem, value = token
            if type(value) is int:
                if value <= self.seen.get(sem.num, 0):
                    continue
                self.seen[sem.num] = value
            self.e.wait_ge(sem, value)


class Core:

    def __init__(self, nc, plan):
        self.nc, self.plan = nc, plan
        self.T = Lane("pe", nc.tensor, nc.alloc_semaphore("pe_steps"))
        self.A = Lane("act", nc.scalar, nc.alloc_semaphore("act_steps"))
        self.V = Lane("dve", nc.vector, nc.alloc_semaphore("dve_steps"))
        self.G = Lane("pool", nc.gpsimd, nc.alloc_semaphore("pool_steps"))
        self.landed = [nc.alloc_semaphore(f"chunk_landed{k}") for k in range(LAND)]
        self.used = nc.alloc_semaphore("chunk_used")
        self.chunk = 0
        self.loops = 0

    def buf(self, name, shape, dtype=F32):
        return self.nc.alloc_sbuf_tensor(name, shape, dtype)

    @contextmanager
    def loop(self, n, lanes):
        self.loops += 1
        me = self.loops
        start = {lane.name: lane.n for lane in lanes}
        per = {lane.name: self.plan.get((me, lane.name), 0) for lane in lanes}
        kind = {"pe": ENG.PE, "act": ENG.Activation, "dve": ENG.DVE, "pool": ENG.Pool}
        with self.nc.Fori(0, n, engines=tuple(kind[lane.name] for lane in lanes)) as i:
            before = {lane.name: lane.turn for lane in lanes}
            for lane in lanes:
                lane.turn = lane.turn + i * per[lane.name]

            def label(name, lane):
                self.plan[me, name] = (lane.n - start[lane.name],)

            def prev(name, lane):
                offset = self.plan.get((me, name), (0,))[0]
                return (lane.sem, lane.turn + (start[lane.name] + offset - per[lane.name]))

            yield i, label, prev
            for lane in lanes:
                steps = lane.n - start[lane.name]
                self.plan[me, lane.name] = steps
                lane.turn = before[lane.name]
                lane.n = start[lane.name] + n * steps


def stream_weights(c, stream, ring):
    sp = c.nc.sync
    n = stream.shape[0]

    body = RING * LAND

    landed_by = sp.alloc_register("sp_landed_by")
    freed_by = sp.alloc_register("sp_freed_by")

    def load(static, turn):
        in_loop = type(turn) is not int
        if in_loop:
            sp.reg_add(freed_by, freed_by, 1)
            if static % LAND == 0:
                sp.reg_add(landed_by, landed_by, 16)
        if in_loop or static >= RING:
            sp.wait_ge(c.used, freed_by if in_loop else static - RING + 1)
        if in_loop or static >= LAND:
            sp.wait_ge(c.landed[static % LAND], landed_by if in_loop else 16 * (static // LAND))
        sp.dma_start(ring[:, static % RING, :], stream[turn * body + static]).then_inc(c.landed[static % LAND], 16)

    first = min(body, n)
    for k in range(first):
        load(k, 0)
    turns = (n - first) // body
    if turns:
        sp.reg_mov(freed_by, first - RING)
        sp.reg_mov(landed_by, 16 * (first // LAND - 1))
        with c.nc.Fori(0, turns, engines=(ENG.SP,)) as r:
            for k in range(body):
                load(first + k, r)
    for k in range(first + turns * body, n):
        load(k, 0)


class Model:
    def __init__(self, c, args):
        nc = c.nc
        self.c, self.a = c, args
        self.T, self.A, self.V, self.G = c.T, c.A, c.V, c.G
        self.ring = c.buf("ring", [P, RING, CHUNK])
        self.consts = c.buf("consts", [P, N_CONST])
        self.cols = c.buf("cols", [P, N_COLS])
        self.rows = c.buf("rows", [P, N_ROWS])
        self.h = c.buf("h", [P, NT + 1, D])
        self.xT = c.buf("xT", [P, KT, KEYS3])
        self.proj = c.buf("proj", [P, 7680])
        self.mix = c.buf("mix", [P, NT, D])
        self.work = c.buf("work", [P, 9216])
        self.logit = c.buf("logit", [P, 2, NT, KEYS3])
        self.probT = c.buf("probT", [P, 2, NT * NT, P])
        self.probM = c.buf("probM", [META, 2, NT, P])
        self.small = c.buf("small", [P, 256])
        self.ps = nc.alloc_psum_tensor("ps", [P, 8, 512], F32)
        self.s_param = nc.alloc_semaphore("params_landed")
        self.params = 0

    def const(self, name, rows=P):
        at, width = CONSTS[name]
        return self.consts[0:rows, at:at + width]

    def col(self, name, k):
        at, _ = COLS[name]
        return self.cols[:, at + k:at + k + 1]

    def row(self, name):
        at, width = ROWS[name]
        return self.rows[:, at:at + width]

    def load(self, dst, src):
        self.A.e.dma_start(dst, src).then_inc(self.s_param, 16)
        self.params += 1
        return (self.s_param, 16 * self.params)

    def fence(self):
        lanes = (self.T, self.A, self.V)
        marks = [lane.now() for lane in lanes if lane.n] + [(self.c.used, self.c.chunk)] * (self.c.chunk > 0)
        for lane in lanes:
            lane.wait(*marks)

    def v(self, make, *after):
        self.V.wait(self.V.now() if self.V.n else None, *after)
        return self.V.did(make(self.V.e))

    def s(self, make, *after):
        self.A.wait(self.A.now() if self.A.n else None, *after)
        return self.A.did(make(self.A.e))

    def rsqrt(self, out, var, scratch, ready):
        root = self.s(lambda e: e.activation(out, var, ACT.Sqrt), ready)
        self.v(lambda e: e.reciprocal(out, out), root)
        self.v(lambda e: e.tensor_tensor(scratch, out, out, ALU.mult))
        self.v(lambda e: e.tensor_tensor(scratch, scratch, var, ALU.mult))
        self.v(lambda e: e.tensor_scalar(scratch, scratch, -0.5, 1.5, ALU.mult, ALU.add))
        return self.v(lambda e: e.tensor_tensor(out, out, scratch, ALU.mult))

    def rms_scale(self, src, tiles, width, ready, eps=1e-6):
        ss, r, tmp = self.small[:, 0:3], self.small[:, 4:7], self.small[:, 8:11]
        if any(rows < P for rows in tiles):
            self.v(lambda e: e.memset(ss, 1.0), ready)
        for t, rows in enumerate(tiles):
            scr = self.work[0:rows, 8192:8192 + width]
            done = self.s(lambda e: e.activation(scr, src(t, rows), ACT.Square,
                                                 accum_out=ss[0:rows, t:t + 1]), ready, self.V.now())
        n = len(tiles)
        done = self.v(lambda e: e.tensor_scalar(ss[:, 0:n], ss[:, 0:n], 1.0 / width, eps, ALU.mult, ALU.add), done)
        self.rsqrt(r[:, 0:n], ss[:, 0:n], tmp[:, 0:n], done)
        return r

    def turn(self, src, tiles, k_tiles, dst, ready, gain=None):
        T, A, V = self.T, self.A, self.V
        ident = self.const("ident")
        freed = [None] * 4
        T.wait(ready, A.now(), V.now())
        width = sum(tiles)
        step = 2 if width <= 256 else 1
        for b, k0 in enumerate(range(0, k_tiles, step)):
            ks = list(range(k0, min(k0 + step, k_tiles)))
            bank = b % 4
            T.wait(freed[bank])
            for n, k in enumerate(ks):
                at = 0
                for t, rows in enumerate(tiles):
                    ins = T.e.transpose(self.ps[0:P, bank, n * width + at:n * width + at + rows],
                                        src(t, rows, k), ident[0:rows, 0:rows])
                    at += rows
            turned = T.did(ins)
            got = self.ps[:, bank, 0:len(ks) * width].rearrange("p (k w) -> p k w", w=width)
            out = dst[:, k0:k0 + len(ks), 0:width]
            if gain is None:
                A.wait(turned)
                done = A.did(A.e.copy(out, got))
            else:
                at, _ = COLS[gain]
                g = self.cols[:, at + k0:at + k0 + len(ks)].unsqueeze(2).to_broadcast([P, len(ks), width])
                V.wait(turned)
                done = V.did(V.e.tensor_tensor(out, got, g, ALU.mult))
            freed[bank] = done
        return done

    def norm_to_xT(self, src, tiles, width, gain, dst, ready):
        r = self.rms_scale(src, tiles, width, ready)
        hn = self.work[:, 0:3 * D].rearrange("p (t d) -> p t d", t=3)
        for t, rows in enumerate(tiles):
            normed = self.v(lambda e: e.tensor_scalar(hn[0:rows, t, 0:width], src(t, rows), r[0:rows, t:t + 1],
                                                      None, ALU.mult))
        return self.turn(lambda t, rows, k: hn[0:rows, t, k * P:(k + 1) * P], tiles, width // P, dst,
                         normed, gain)

    def final_norm(self, gain, ready):
        r = self.rms_scale(lambda t, rows: self.h[0:rows, t, :], [P] * NT, D, ready)
        for t in range(NT):
            done = self.v(lambda e: e.scalar_tensor_tensor(self.h[:, t, :], self.h[:, t, :], r[:, t:t + 1],
                                                           self.row(gain), ALU.mult, ALU.mult))
        return done

    def chunk_at(self, k, static):
        if type(k) is int:
            return lambda lo, n: self.ring[:, k % RING, lo:lo + n]
        flat = self.ring[:, :, :].rearrange("p r c -> p (r c)")
        slot = self.T.e.snap((k % RING) * CHUNK)
        return lambda lo, n: flat[:, ds(slot + lo, n)]

    def wait_chunk(self, static, k):
        turns = (k - static) // LAND if type(k) is not int else 0
        value = (static // LAND + 1) * 16
        if type(k) is not int:
            value = self.loop_turn * 16 + value
        self.T.wait((self.c.landed[static % LAND], value))

    def linear(self, n_chunks, tiles, evac, ready, k_tiles=KT, width=CW, xT=None):
        c, T = self.c, self.T
        xT = self.xT if xT is None else xT
        T.wait(ready)
        self.fence()
        last = {}

        def one(j, first, k, number):
            self.wait_chunk(first, k)
            at = self.chunk_at(k, first)
            for t, rows in enumerate(tiles):
                out = self.ps[0:rows, j, t * width:(t + 1) * width] if t < NT else \
                    self.ps[0:rows, 3 + j, 0:width]
                for kt in range(k_tiles):
                    ins = T.e.matmul(out, xT[:, kt, t * P:t * P + rows], at(kt * width, width),
                                     start=(kt == 0), stop=(kt == k_tiles - 1))
            ins.then_inc(c.used, 1)
            products = (c.used, k + 1)
            return evac(j, number, products)

        c0 = c.chunk
        turns = n_chunks // 3
        done = None
        if turns > 1:
            with c.loop(turns, (T, self.A, self.V)) as (i, label, prev):
                self.loop_turn = i
                for j in range(3):
                    T.wait(prev(f"bank{j}", self.evac_lane))
                    one(j, c0 + j, i * 3 + (c0 + j), i * 3 + j)
                    label(f"bank{j}", self.evac_lane)
            number = 3 * turns
            done = self.evac_lane.now()
            T.wait(done)
        else:
            number = 0
        for m in range(number, n_chunks):
            T.wait(last.get(m % 3))
            done = one(m % 3, c0 + m, c0 + m, m)
            last[m % 3] = done
        c.chunk = c0 + n_chunks
        return done

    def to(self, dst, func=None):
        self.evac_lane = self.A
        A = self.A

        def evac(j, number, products, meta=True):
            A.wait(products)
            cols = ds(number * CW, CW) if type(number) is not int else slice(number * CW, (number + 1) * CW)
            got = self.ps[:, j, :].rearrange("p (t w) -> p t w", t=NT)
            if func is None:
                ins = A.e.copy(dst[:, 0:NT, cols], got)
            else:
                ins = A.e.activation(dst[:, 0:NT, cols], got, func)
            done = A.did(ins)
            if self.with_meta:
                done = A.did(A.e.copy(dst[0:META, NT, cols], self.ps[0:META, 3 + j, 0:CW]))
            return done
        return evac

    with_meta = False

    def add_to_h(self):
        self.evac_lane = self.V
        V = self.V

        def evac(j, number, products):
            V.wait(products)
            cols = ds(number * CW, CW) if type(number) is not int else slice(number * CW, (number + 1) * CW)
            got = self.ps[:, j, :].rearrange("p (t w) -> p t w", t=NT)
            return V.did(V.e.tensor_tensor(self.h[:, 0:NT, cols], self.h[:, 0:NT, cols], got, ALU.add))
        return evac

    def swiglu(self, groups, ready, gates=None):
        c, T, A, V, ps = self.c, self.T, self.A, self.V, self.ps
        act = self.work[:, 0:512].rearrange("p (f t w) -> p f t w", f=2, t=NT)
        silu = self.work[:, 1024:1536].rearrange("p (f t w) -> p f t w", f=2, t=NT)
        actT = self.work[:, 1536:2048].rearrange("p (f t w) -> p f t w", f=2, t=NT)
        ident = self.const("ident")
        T.wait(ready)
        self.fence()
        c0 = c.chunk
        hidden = self.ps[:, 4:6, :].rearrange("p f (t m w) -> p f t m w", t=NT, m=2)

        def up(f, static, k):
            self.wait_chunk(static, k)
            at = self.chunk_at(k, static)
            for t in range(NT):
                for kt in range(KT):
                    ins = T.e.matmul(ps[:, 4 + f, t * CW:(t + 1) * CW], self.xT[:, kt, t * P:(t + 1) * P],
                                     at(kt * CW, CW), start=(kt == 0), stop=(kt == KT - 1))
            ins.then_inc(c.used, 1)
            return (c.used, k + 1)

        def activate(f, products, group, turned):
            A.wait(products, V.now())
            s = A.did(A.e.activation(silu[:, f, :, :], hidden[:, f, :, 0, :], ACT.Silu))
            V.wait(s, turned)
            if gates is None:
                return V.did(V.e.tensor_tensor(act[:, f, :, :], hidden[:, f, :, 1, :], silu[:, f, :, :], ALU.mult))
            for t in range(NT):
                g = gates[:, t, group:group + 1] if type(group) is int else gates[:, t, ds(group, 1)]
                done = V.did(V.e.scalar_tensor_tensor(act[:, f, t, :], hidden[:, f, t, 1, :], g,
                                                      silu[:, f, t, :], ALU.mult, ALU.mult))
            return done

        def transpose(f, acted, left):
            T.wait(acted, left)
            for t in range(NT):
                ins = T.e.transpose(ps[:, 6 + f, t * P:(t + 1) * P], act[:, f, t, :], ident)
            turned = T.did(ins)
            A.wait(turned)
            return turned, A.did(A.e.copy(actT[:, f, :, :], ps[:, 6 + f, 0:SEQ].rearrange("p (t w) -> p t w", t=NT)))

        def down(f, copied, at):
            T.wait(copied)
            for t in range(NT):
                for half in range(2):
                    ins = T.e.matmul(ps[:, 2 * t + half, :], actT[:, f, t, :], at(f * D + half * 512, 512),
                                     start=False, stop=False, skip_group_check=True)
            return ins

        zero = self.small[0:1, 64:192]
        zeros = self.logit[0:1, 0, :, :].rearrange("p a b -> p (a b)")[:, 0:512]
        V.did(V.e.memset(zero, 0.0))
        zeroed = V.did(V.e.memset(zeros, 0.0))
        T.wait(zeroed)
        for b in range(4):
            T.e.matmul(ps[:, b, :], zero, zeros, start=True, stop=False, skip_group_check=True)

        h0 = up(0, c0, c0)
        activate(0, h0, 0, None)
        h1 = up(1, c0 + 1, c0 + 1)
        activate(1, h1, 0, None)
        with c.loop(groups - 1, (T, A, V)) as (i, label, prev):
            self.loop_turn = i
            base = c0 + 2
            acted = V.now()
            k = i * 3 + base
            group = i + 1
            w2 = None
            for f in range(2):
                T.wait(prev(f"act{f}", V))
                products = up(f, base + f, k + f)
                turned, copied = transpose(f, acted, A.now())
                activate(f, products, group, turned)
                label(f"act{f}", V)
                if w2 is None:
                    self.wait_chunk(base + 2, k + 2)
                    w2 = self.chunk_at(k + 2, base + 2)
                ins = down(f, copied, w2)
            ins.then_inc(c.used, 1)
        last = c0 + 3 * groups - 1
        for f in range(2):
            turned, copied = transpose(f, V.now(), A.now())
            if f == 0:
                self.wait_chunk(last, last)
            ins = down(f, copied, self.chunk_at(last, last))
        for b in range(4):
            ins2 = T.e.matmul(ps[:, b, :], zero, zeros, start=False, stop=True, skip_group_check=True)
        ins2.then_inc(c.used, 1)
        c.chunk = c0 + 3 * groups
        V.wait((c.used, c.chunk))
        for t in range(NT):
            done = V.did(V.e.tensor_tensor(self.h[:, t, :], self.h[:, t, :],
                                           ps[:, 2 * t:2 * t + 2, :].rearrange("p b w -> p (b w)"), ALU.add))
        return done

    def attend(self, heads, dh, nk, q, k, values, blocks, scale, bias, out, dv, ready, sink=None):
        T, A, V, ps = self.T, self.A, self.V, self.ps
        ident = self.const("ident")
        nmax = self.small[:, 64:96].rearrange("p (h t) -> p h t", t=NT)
        total = self.small[:, 96:128].rearrange("p (h t) -> p h t", t=NT)
        extra = self.small[:, 128:160].rearrange("p (h t) -> p h t", t=NT)
        whole = [b for b in range(len(blocks)) if blocks[b][1] == P]
        T.wait(*ready)
        self.fence()
        soft, scored, turned, spread, outed, weighed = {}, {}, {}, {}, {}, {}

        def scores(h):
            L = self.logit[:, h % 2, :, 0:nk]
            T.wait(scored.get(h - 2))
            for t in range(NT):
                ins = T.e.matmul(ps[:, 2 * (h % 2) + t, 0:nk], q(h, t), k(h), start=True, stop=True)
            s = T.did(ins)
            V.wait(s, turned.get(h - 2), *ready)
            scored[h] = V.did(V.e.scalar_tensor_tensor(L, ps[:, 2 * (h % 2):2 * (h % 2) + 2, 0:nk], scale,
                                                       bias(h), ALU.mult, ALU.add))
            V.wait(scored[h])
            top = V.did(V.e.tensor_reduce(nmax[:, h, :], L, AX_X, ALU.max, negate=True))
            if sink is not None:
                V.wait(top)
                V.did(V.e.tensor_scalar(extra[:, h, :], nmax[:, h, :], -1.0, sink(h), ALU.mult, ALU.max))
                V.wait(V.now())
                top = V.did(V.e.tensor_scalar(nmax[:, h, :], extra[:, h, :], -1.0, None, ALU.mult))
            A.wait(top)
            for t in range(NT):
                done = A.did(A.e.activation(L[:, t, :], L[:, t, :], ACT.Exp, bias=nmax[:, h, t:t + 1],
                                            accum_out=total[:, h, t:t + 1]))
            if sink is not None:
                done = A.did(A.e.activation(extra[:, h, :], nmax[:, h, :], ACT.Exp, bias=sink(h)))
            soft[h] = done

        def transpose(h):
            L = self.logit[:, h % 2, :, :]
            bank = 4 + 2 * (h % 2)
            T.wait(soft[h], spread.get(h - 2), outed.get(h - 2))
            for t in range(NT):
                for n, b in enumerate(whole):
                    col = blocks[b][0]
                    ins = T.e.transpose(ps[:, bank, (t * NT + n) * P:(t * NT + n + 1) * P],
                                        L[:, t, col:col + P], ident)
                for b, (col, rows) in enumerate(blocks):
                    if rows < P:
                        ins = T.e.transpose(ps[0:rows, bank + 1, t * P:(t + 1) * P],
                                            L[:, t, col:col + rows], ident)
            turned[h] = T.did(ins)
            A.wait(turned[h], weighed.get(h - 2))
            done = A.did(A.e.copy(self.probT[:, h % 2, :, :].rearrange("p b w -> p (b w)"), ps[:, bank, :]))
            if len(blocks) > len(whole):
                done = A.did(A.e.copy(self.probM[:, h % 2, :, :].rearrange("p b w -> p (b w)"),
                                      ps[0:META, bank + 1, 0:NT * P]))
            spread[h] = done

        def weigh(h):
            bank = 5 + 2 * (h % 2)
            T.wait(spread[h])
            for t in range(NT):
                for b, (col, rows) in enumerate(blocks):
                    left = self.probT[:, h % 2, t * NT + whole.index(b), :] if rows == P else \
                        self.probM[:, h % 2, t, :]
                    ins = T.e.matmul(ps[:, bank, 256 + t * dv:256 + (t + 1) * dv], left, values(h, b),
                                     start=(b == 0), stop=(b == len(blocks) - 1))
            weighed[h] = T.did(ins)
            if sink is not None:
                V.wait(soft[h])
                V.did(V.e.tensor_tensor(total[:, h, :], total[:, h, :], extra[:, h, :], ALU.add))
                V.wait(V.now())
            V.wait(soft[h])
            V.did(V.e.reciprocal(total[:, h, :], total[:, h, :]))
            V.wait(V.now(), weighed[h])
            got = ps[:, bank, 256:256 + NT * dv].rearrange("p (t w) -> p t w", t=NT)
            outed[h] = V.did(V.e.tensor_tensor(out(h), got, total[:, h, :].unsqueeze(2).to_broadcast([P, NT, dv]),
                                               ALU.mult))

        for s in range(heads + 2):
            if s < heads:
                scores(s)
            if 0 <= s - 1 < heads:
                transpose(s - 1)
            if s >= 2:
                weigh(s - 2)
        return self.V.now()

    def turn_heads(self, jobs, ready):
        T, A, V = self.T, self.A, self.V
        ident = self.const("ident")
        freed = [None] * 4
        T.wait(*ready, A.now(), V.now())
        for n, (sources, dst) in enumerate(jobs):
            bank = n % 4
            T.wait(freed[bank])
            at = 0
            for src, rows in sources:
                width = src.shape[-1]
                ins = T.e.transpose(self.ps[0:width, bank, at:at + rows], src, ident[0:rows, 0:rows])
                at += rows
            done = T.did(ins)
            lane = A if n % 2 else V
            lane.wait(done)
            got = self.ps[0:width, bank, 0:at]
            freed[bank] = A.did(A.e.copy(dst, got)) if lane is A else V.did(V.e.tensor_copy(dst, got))
        return A.now(), V.now()

    def product(self, k_tiles, cols, tiles, xT, evac):
        c, T = self.c, self.T
        self.fence()
        k = c.chunk
        self.wait_chunk(k, k)
        at = self.chunk_at(k, k)
        for n in range(cols // CW):
            for t, rows in enumerate(tiles):
                out = self.ps[0:rows, n, t * CW:(t + 1) * CW] if t < NT else self.ps[0:rows, 4 + n, 0:CW]
                for kt in range(k_tiles):
                    ins = T.e.matmul(out, xT[:, kt, t * P:t * P + rows], at(kt * cols + n * CW, CW),
                                     start=(kt == 0), stop=(kt == k_tiles - 1))
            if n < cols // CW - 1:
                done = evac(n, T.did(ins))
        ins.then_inc(c.used, 1)
        c.chunk += 1
        return evac(cols // CW - 1, (c.used, c.chunk))

    def set_up(self):
        a, c = self.a, self.c
        self.load(self.consts[:, :], a["consts"])
        self.load(self.cols[:, :], a["cols"])
        self.load(self.h[:, 0:NT, :], a["x"].rearrange("b (t p) d -> p (b t) d", p=P))
        self.load(self.rows[:, :], a["rows"].to_broadcast([P, N_ROWS]))
        self.load(self.h[0:META, NT, :], a["meta_tokens_3"])
        self.load(self.work[0:33, 0:1024], a["buckets"])
        rel = self.small[0:33, 192:200]
        masked = self.V.did(self.V.e.memset(rel, NEG))
        self.A.wait(masked)
        return self.load(self.small[0:32, 192:200], a["rel_bias"])

    def bias_vectors(self, ready):
        T, A = self.T, self.A
        T.wait(ready)
        for kind in range(2):
            ins = T.e.matmul(self.ps[0:8, kind, :], self.small[0:33, 192:200],
                             self.work[0:33, kind * 512:(kind + 1) * 512], start=True, stop=True)
        made = T.did(ins)
        A.wait(made)
        flat = self.mix[0:8, 0, 0:1024]
        copied = A.did(A.e.copy(flat, self.ps[0:8, 0:2, :].rearrange("p b w -> p (b w)")))
        A.wait(copied)
        for kind in range(2):
            stored = self.load(self.u[kind], self.mix[0:8, 0, kind * 512:(kind + 1) * 512])
        A.wait(stored)
        return stored

    def bias_tiles(self, kind, dst):
        T, A, V = self.T, self.A, self.V
        shifted = self.mix[:, :, :].rearrange("p t d -> p (t d)")
        for t in range(NT):
            self.fence()
            src = bass.AP(tensor=self.u.tensor, offset=kind * 8 * 512 + (1 - t) * P, ap=[[1, P], [512, 8], [1, SEQ]])
            loaded = self.load(shifted.rearrange("p (h k) -> p h k", h=8), src)
            T.wait(loaded)
            for b in range(4):
                ins = T.e.matmul(self.ps[:, b, :], self.const("flip"), shifted[:, b * 512:(b + 1) * 512],
                                 start=True, stop=True)
            made = T.did(ins)
            for b in range(4):
                lane = A if b % 2 else V
                lane.wait(made)
                out = dst[:, t, 2 * b:2 * b + 2, :].rearrange("p h k -> p (h k)")
                if lane is A:
                    A.did(A.e.copy(out, self.ps[:, b, :]))
                else:
                    V.did(V.e.tensor_copy(out, self.ps[:, b, :]))
        self.fence()

    def head_rms(self, buf, heads, gain, factor, ready):
        n = NT * heads
        view = buf.rearrange("p t (h e) -> p t h e", h=heads)
        sq = self.work[:, 4096:4096 + n * P].rearrange("p (t h e) -> p t h e", t=NT, h=heads)
        ss, r, tmp = self.small[:, 12:12 + n], self.small[:, 20:20 + n], self.small[:, 28:28 + n]
        self.v(lambda e: e.tensor_tensor(sq, view, view, ALU.mult), ready)
        self.v(lambda e: e.tensor_reduce(ss, self.work[:, 4096:4096 + n * P].rearrange("p (g e) -> p g e", e=P),
                                         AX_X, ALU.add))
        ms = self.v(lambda e: e.tensor_scalar(ss, ss, 1.0 / P, 1e-6, ALU.mult, ALU.add))
        self.rsqrt(r, ss, tmp, ms)
        rb = r.rearrange("p (t h) -> p t h", t=NT).unsqueeze(3).to_broadcast([P, NT, heads, P])
        self.v(lambda e: e.tensor_tensor(view, view, rb, ALU.mult))
        for t in range(NT):
            gb = self.row(gain).unsqueeze(1).to_broadcast([P, heads, P])
            done = self.v(lambda e: e.scalar_tensor_tensor(view[:, t], view[:, t], factor, gb, ALU.mult, ALU.mult))
        return done

    def gla(self, pr):
        T, A, V, ps, w = self.T, self.A, self.V, self.ps, self.work
        H = 4

        def area(at, *shape):
            n = 1
            for s in shape:
                n *= s
            names = "abc"[:len(shape)]
            spec = " ".join(names)
            v = w[:, at:at + n]
            return v if len(shape) == 1 else v.rearrange(f"p ({spec}) -> p {spec}", **dict(zip(names, shape)))

        qeT, keT = area(0, H, SEQ), area(1024, H, SEQ)
        kd = area(2048, NT, 256)
        g = area(2560, NT, 256)
        t1, t2, t3 = area(3072, NT, 256), area(3584, NT, 256), area(4096, NT, 256)
        qe, ke = area(4608, NT, 256), area(5120, NT, 256)
        state = area(5632, 3, H * P)
        up, downT = w[0:17, 7168:7424], w[0:17, 7424:7680]
        attT = w[:, 7680:8704].rearrange("p (h t c) -> p h t c", h=H, t=NT)
        decay = w[0:64, 8704:8720]
        self.fence()
        up_loaded = self.load(up, self.a["gla_up"])
        ones = V.did(V.e.memset(downT, 1.0))
        zeroed = V.did(V.e.memset(attT, 0.0))
        A.wait(ones)
        V.wait(ones)
        d = self.turn_heads([([(pr[:, t, 2816:2832], P) for t in range(NT)], downT[0:16, :])], ())
        T.wait(*d, up_loaded)
        for t in range(NT):
            ins = T.e.matmul(ps[:, 4, t * 256:(t + 1) * 256], downT[:, t * P:(t + 1) * P], up, start=True, stop=True)
        z_made = T.did(ins)
        z = ps[:, 4, :].rearrange("p (t w) -> p t w", t=NT)
        read = self.s(lambda e: e.activation(t1, z, ACT.Abs), z_made)
        self.v(lambda e: e.tensor_scalar(g, z, 0.0, None, ALU.min), read)
        self.s(lambda e: e.activation(t1, t1, ACT.Exp, scale=-1.0))
        logged = self.s(lambda e: e.activation(t1, t1, ACT.Ln, bias=1.0))
        self.v(lambda e: e.tensor_tensor(g, g, t1, ALU.subtract), logged)
        gated = self.v(lambda e: e.tensor_scalar(g, g, 1.0 / 16.0, None, ALU.mult))
        T.wait(gated)
        for t in range(NT):
            T.e.matmul(ps[:, 5, t * 256:(t + 1) * 256], self.const("tri"), g[:, t, :], start=True, stop=True)
            T.e.matmul(ps[:, 6, t * 256:(t + 1) * 256], self.const("same"), g[:, t, :], start=True, stop=True)
            for h in range(H):
                ins = T.e.matmul(ps[0:64, 7, (h * NT + t) * 2:(h * NT + t) * 2 + 2],
                                 g[:, t, h * 64:(h + 1) * 64], self.const("half"), start=True, stop=True)
        summed = T.did(ins)
        b = ps[:, 5, :].rearrange("p (t w) -> p t w", t=NT)
        b_last = ps[:, 6, :].rearrange("p (t w) -> p t w", t=NT)
        self.s(lambda e: e.copy(t3, b), summed)
        self.s(lambda e: e.activation(t1, b, ACT.Exp))
        self.s(lambda e: e.activation(t2, b, ACT.Exp, scale=-1.0))
        exps = self.s(lambda e: e.activation(decay, ps[0:64, 7, 0:16], ACT.Exp))
        self.v(lambda e: e.scalar_tensor_tensor(qe, pr[:, :, 0:256], 64 ** -0.5, t1, ALU.mult, ALU.mult), exps)
        self.v(lambda e: e.tensor_tensor(ke, pr[:, :, 256:512], t2, ALU.mult))
        left = self.v(lambda e: e.tensor_tensor(t3, b_last, t3, ALU.subtract))
        ends = self.s(lambda e: e.activation(t3, t3, ACT.Exp), left)
        kd_made = self.v(lambda e: e.tensor_tensor(kd, pr[:, :, 256:512], t3, ALU.mult), ends)
        jobs = []
        for src, dst in ((qe, qeT), (ke, keT)):
            for h in (0, 2):
                jobs.append(([(src[:, t, (h + u) * 64:(h + u + 1) * 64], P) for u in range(2) for t in range(NT)],
                             dst[0:64, h:h + 2, :].rearrange("p h w -> p (h w)")))
        d = self.turn_heads(jobs, (kd_made,))
        T.wait(*d)
        for h in range(H):
            for t in range(NT):
                ins = T.e.matmul(ps[:, h, t * P:(t + 1) * P], keT[0:64, h, t * P:(t + 1) * P],
                                 qeT[0:64, h, t * P:(t + 1) * P], start=True, stop=True)
        scored = T.did(ins)
        V.wait(scored, zeroed)
        mask = self.const("tri").bitcast(U32).unsqueeze(1).to_broadcast([P, NT, P])
        for h in range(H):
            kept = V.did(V.e.copy_predicated(attT[:, h], mask, ps[:, h, 0:256].rearrange("p (t c) -> p t c", t=NT)))
        for n in range(3):
            t, lo = n // 2, 64 * (n % 2)
            for h in range(H):
                ins = T.e.matmul(ps[0:64, 4 + n, h * P:(h + 1) * P], kd[lo:lo + 64, t, h * 64:(h + 1) * 64],
                                 pr[lo:lo + 64, t, 512 + h * P:512 + (h + 1) * P], start=True, stop=True)
        added = T.did(ins)
        self.v(lambda e: e.tensor_copy(state[0:64, 0, :], ps[0:64, 4, :]), added)
        for n in (1, 2):
            for h in range(H):
                k = (h * NT + n // 2) * 2 + n % 2
                states = self.v(lambda e: e.scalar_tensor_tensor(
                    state[0:64, n, h * P:(h + 1) * P], state[0:64, n - 1, h * P:(h + 1) * P], decay[:, k:k + 1],
                    ps[0:64, 4 + n, h * P:(h + 1) * P], ALU.mult, ALU.add))
        T.wait(kept, states)
        for h in range(H):
            for t in range(NT):
                T.e.matmul(ps[:, h, t * P:(t + 1) * P], attT[:, h, t, :], pr[:, t, 512 + h * P:512 + (h + 1) * P],
                           start=True, stop=False, skip_group_check=True)
                for half in range(2):
                    n = 2 * t + half
                    if n:
                        lo = 64 * half
                        ins = T.e.matmul(ps[lo:lo + 64, h, t * P:(t + 1) * P], qeT[0:64, h, n * 64:(n + 1) * 64],
                                         state[0:64, n - 1, h * P:(h + 1) * P], start=False, stop=(half == 1),
                                         skip_group_check=True)
        made = T.did(ins)
        out = self.mix[:, :, 0:512]
        for t in range(NT):
            copied = self.s(lambda e: e.copy(self.mix[:, t, 0:512].rearrange("p (h e) -> p h e", h=H),
                                             ps[:, 0:H, t * P:(t + 1) * P]), made)
        self.fence()
        return self.head_rms(out, H, "gla", 1.0, copied)

    def gate_and_turn(self, cols, gates, ready):
        lo, hi = cols
        s = self.s(lambda e: e.activation(gates, gates, ACT.Silu), ready)
        return self.v(lambda e: e.tensor_tensor(self.mix[:, :, lo:hi], self.mix[:, :, lo:hi], gates, ALU.mult), s)

    def mix_to_xT(self, ready, tiles_k=KT):
        return self.turn(lambda t, rows, k: self.mix[0:rows, t, k * P:(k + 1) * P], [P] * NT, tiles_k,
                         self.xT, ready)

    def h_tile(self, t, rows):
        return self.h[0:rows, t, :]

    def block1(self, ready):
        w, two = self.work, [P] * NT
        pr = self.proj[:, 0:2 * 3072].rearrange("p (t c) -> p t c", t=NT)
        bias = w[:, 0:4096].rearrange("p (t h k) -> p t h k", t=NT, h=8)
        qT = w[:, 4096:6144].rearrange("p (h s) -> p h s", h=8)
        kT = w[:, 6144:6656].rearrange("p (h s) -> p h s", h=2)
        normed = self.norm_to_xT(self.h_tile, two, D, "norm0", self.xT, ready)
        projected = self.linear(N_IN1, two, self.to(pr), normed)
        self.gla(pr)
        self.fence()
        self.bias_scratch_wait()
        saved = self.save_mix()
        self.bias_tiles(1, bias)
        self.restore_mix(saved)
        jobs = []
        for h in range(0, 8, 2):
            jobs.append(([(pr[:, t, 1536 + (h + u) * 64:1536 + (h + u + 1) * 64], P) for u in range(2)
                          for t in range(NT)], qT[0:64, h:h + 2, :].rearrange("p h s -> p (h s)")))
        jobs.append(([(pr[:, t, 2048 + u * 64:2048 + (u + 1) * 64], P) for u in range(2) for t in range(NT)],
                     kT[0:64, :, :].rearrange("p h s -> p (h s)")))
        turned = self.turn_heads(jobs, ())
        sinks = self.row("sinks")
        self.attend(8, 64, SEQ, lambda h, t: qT[0:64, h, t * P:(t + 1) * P], lambda h: kT[0:64, h // 4, :],
                    lambda h, b: pr[:, b, 2176 + (h // 4) * 64:2176 + (h // 4 + 1) * 64],
                    [(0, P), (P, P)], 64 ** -0.5, lambda h: bias[:, :, h, :],
                    lambda h: self.mix[:, :, 512 + h * 64:512 + (h + 1) * 64], 64, turned,
                    sink=lambda h: sinks[:, h:h + 1])
        self.fence()
        self.gate_and_turn((0, 512), pr[:, :, 1024:1536], None)
        mixed = self.gate_and_turn((512, 1024), pr[:, :, 2304:2816], None)
        self.linear(N_OUT, two, self.add_to_h(), self.mix_to_xT(mixed))
        self.fence()
        normed = self.norm_to_xT(self.h_tile, two, D, "norm1", self.xT, self.V.now())
        pr = self.proj[:, 0:2 * 2560].rearrange("p (t c) -> p t c", t=NT)
        self.linear(N_ODD, two, self.to(pr), normed)
        self.bias_tiles(0, bias)
        jobs = []
        for h in range(0, 8, 2):
            jobs.append(([(pr[:, t, (h + u) * P:(h + u + 1) * P], P) for u in range(2) for t in range(NT)],
                         qT[:, h:h + 2, :].rearrange("p h s -> p (h s)")))
        jobs.append(([(pr[:, t, 1024 + u * P:1024 + (u + 1) * P], P) for u in range(2) for t in range(NT)],
                     kT[:, :, :].rearrange("p h s -> p (h s)")))
        turned = self.turn_heads(jobs, ())
        self.attend(8, P, SEQ, lambda h, t: qT[:, h, t * P:(t + 1) * P], lambda h: kT[:, h // 4, :],
                    lambda h, b: pr[:, b, 1280 + (h // 4) * P:1280 + (h // 4 + 1) * P],
                    [(0, P), (P, P)], P ** -0.5, lambda h: bias[:, :, h, :],
                    lambda h: self.mix[:, :, h * P:(h + 1) * P], P, turned)
        self.fence()
        mixed = self.gate_and_turn((0, 1024), pr[:, :, 1536:2560], None)
        added = self.linear(N_OUT, two, self.add_to_h(), self.mix_to_xT(mixed))
        self.fence()
        return self.final_norm("final1", added)

    def bias_scratch_wait(self):
        pass

    def save_mix(self):
        aside = self.work[:, 8192:9216].rearrange("p (t c) -> p t c", t=NT)
        return self.v(lambda e: e.tensor_copy(aside, self.mix[:, :, 0:512]))

    def restore_mix(self, saved):
        aside = self.work[:, 8192:9216].rearrange("p (t c) -> p t c", t=NT)
        self.v(lambda e: e.tensor_copy(self.mix[:, :, 0:512], aside), saved)

    def angles(self, ready):
        sm = self.small
        pos_i = sm[:, 200:202].bitcast(I32)
        pos, ang = sm[:, 202:204], self.work[:, 6144:6160].rearrange("p (t f) -> p t f", t=NT)
        out = self.work[:, 6160:6192].rearrange("p (c t f) -> p c t f", c=2, t=NT)
        k = self.work[:, 6192:6208].rearrange("p (t f) -> p t f", t=NT)
        loaded = self.load(pos_i, self.a["positions"])
        self.v(lambda e: e.tensor_copy(pos, pos_i), loaded)
        for t in range(NT):
            self.v(lambda e: e.tensor_scalar(ang[:, t, :], self.row("freq"), pos[:, t:t + 1], None, ALU.mult))
        big = 12582912.0
        for c, shift in ((0, 0.25), (1, 0.0)):
            self.v(lambda e: e.tensor_scalar(k, ang, 1.0 / (2 * PI), shift, ALU.mult, ALU.add))
            self.v(lambda e: e.tensor_scalar(k, k, big, None, ALU.add))
            self.v(lambda e: e.tensor_scalar(k, k, big, None, ALU.subtract))
            o = out[:, c]
            self.v(lambda e: e.scalar_tensor_tensor(o, k, -6.28125, ang, ALU.mult, ALU.add))
            self.v(lambda e: e.scalar_tensor_tensor(o, k, -0.0019350051879882812, o, ALU.mult, ALU.add))
            self.v(lambda e: e.scalar_tensor_tensor(o, k, -3.0199159819567e-07, o, ALU.mult, ALU.add))
            self.v(lambda e: e.tensor_scalar(o, o, shift * 2 * PI, 3.1415925, ALU.add, ALU.min))
            reduced = self.v(lambda e: e.tensor_scalar(o, o, -3.1415925, None, ALU.max))
        done = self.s(lambda e: e.activation(out, out, ACT.Sin), reduced)
        return out[:, 0], out[:, 1], done

    def rope(self, x1, x2, cos, sin, shape, scratch, ready):
        n = 1
        for s in shape:
            n *= s
        rows = x1.shape[0]
        spec = "p (h f) -> p h f"
        ta, tb, tc, td = (scratch[0:rows, k * n:(k + 1) * n].rearrange(spec, f=shape[1]) for k in range(4))
        self.v(lambda e: e.tensor_tensor(ta, x1, cos, ALU.mult), ready)
        self.v(lambda e: e.tensor_tensor(tb, x2, sin, ALU.mult))
        self.v(lambda e: e.tensor_tensor(tc, x2, cos, ALU.mult))
        self.v(lambda e: e.tensor_tensor(td, x1, sin, ALU.mult))
        self.v(lambda e: e.tensor_tensor(x1, ta, tb, ALU.subtract))
        return self.v(lambda e: e.tensor_tensor(x2, tc, td, ALU.add))

    def diff_attention(self, pr):
        w, sm = self.work, self.small
        self.fence()
        cos, sin, made = self.angles(None)
        qk = pr[:, :, 0:1024].rearrange("p t (h d) -> p t h d", d=64)
        for t in range(NT):
            self.rope(qk[:, t, :, 0:8], qk[:, t, :, 8:16], cos[:, t].unsqueeze(1).to_broadcast([P, 16, 8]),
                      sin[:, t].unsqueeze(1).to_broadcast([P, 16, 8]), (16, 8), w[:, 4096:4608], made)
        self.fence()
        qT = w[:, 0:2048].rearrange("p (h s) -> p h s", h=8)
        kT = w[:, 2048:4096].rearrange("p (h s) -> p h s", h=8)
        both = w[:, 4096:6144].rearrange("p (t h c e) -> p t h c e", t=NT, h=4, c=2)
        jobs = []
        for base, dst in ((0, qT), (512, kT)):
            for h in range(0, 8, 2):
                jobs.append(([(pr[:, t, base + (h + u) * 64:base + (h + u + 1) * 64], P) for u in range(2)
                              for t in range(NT)], dst[0:64, h:h + 2, :].rearrange("p h s -> p (h s)")))
        turned = self.turn_heads(jobs, ())
        causal = self.const("causal").rearrange("p (t k) -> p t k", t=NT)
        self.attend(8, 64, SEQ, lambda h, t: qT[0:64, h, t * P:(t + 1) * P], lambda h: kT[0:64, h, :],
                    lambda h, b: pr[:, b, 1024 + (h // 2) * P:1024 + (h // 2 + 1) * P],
                    [(0, P), (P, P)], 64 ** -0.5, lambda h: causal,
                    lambda h: both[:, :, h // 2, h % 2, :], P, turned)
        lam = self.row("lambda").rearrange("p (a b d) -> p a b d", a=2, b=2)
        prod = self.logit[:, 0, 0, 0:128].rearrange("p (a d) -> p a d", a=2)
        self.fence()
        self.v(lambda e: e.tensor_tensor(prod, lam[:, :, 0, :], lam[:, :, 1, :], ALU.mult))
        dots = self.v(lambda e: e.tensor_reduce(sm[:, 204:206], prod, AX_X, ALU.add))
        exped = self.s(lambda e: e.activation(sm[:, 204:206], sm[:, 204:206], ACT.Exp), dots)
        self.v(lambda e: e.tensor_tensor(sm[:, 206:207], sm[:, 205:206], sm[:, 204:205], ALU.subtract), exped)
        self.v(lambda e: e.tensor_scalar(sm[:, 206:207], sm[:, 206:207], 0.8 - 0.6, None, ALU.subtract))
        out = self.mix[:, :, 0:512].rearrange("p t (h e) -> p t h e", h=4)
        for t in range(NT):
            self.v(lambda e: e.scalar_tensor_tensor(out[:, t], both[:, t, :, 1, :], sm[:, 206:207],
                                                    both[:, t, :, 0, :], ALU.mult, ALU.add))
        self.fence()
        return self.head_rms(self.mix[:, :, 0:512], 4, "subln", 1.0 - (0.8 - 0.6), self.V.now())

    def conv(self, pr):
        w = self.work
        self.fence()
        z = self.mix[:, :, 512:1024]
        zT = w[:, 0:4 * 258].rearrange("p (k s) -> p k s", k=4)
        bT = w[:, 1032:1032 + 1024].rearrange("p (k s) -> p k s", k=4)
        self.v(lambda e: e.memset(w[:, 0:4 * 258], 0.0))
        made = self.v(lambda e: e.tensor_tensor(z, pr[:, :, 2048:2560], pr[:, :, 2560:3072], ALU.mult))
        self.A.wait(made)
        self.turn(lambda t, rows, k: z[:, t, k * P:(k + 1) * P], [P] * NT, 4, zT[:, :, 2:258], made)
        done = self.turn(lambda t, rows, k: pr[:, t, 1536 + k * P:1536 + (k + 1) * P], [P] * NT, 4, bT,
                         self.A.now())
        self.V.wait(done)
        for k in range(4):
            o = self.xT[:, 4 + k, 0:SEQ]
            self.v(lambda e: e.tensor_scalar(o, zT[:, k, 0:SEQ], self.col("conv", k), None, ALU.mult), done)
            self.v(lambda e: e.scalar_tensor_tensor(o, zT[:, k, 1:257], self.col("conv", 4 + k), o, ALU.mult, ALU.add))
            self.v(lambda e: e.scalar_tensor_tensor(o, zT[:, k, 2:258], self.col("conv", 8 + k), o, ALU.mult, ALU.add))
        return self.v(lambda e: e.tensor_tensor(self.xT[:, 4:8, 0:SEQ], self.xT[:, 4:8, 0:SEQ], bT, ALU.mult))

    def ple(self, layer):
        V = self.V
        two = [P] * NT
        self.fence()
        p_tm = self.work[:, 7168:7680].rearrange("p (t c) -> p t c", t=NT)
        pT = self.work[:, 7680:8192].rearrange("p (k s) -> p k s", k=2)
        p_loaded = self.load(p_tm, self.a["p_2"][layer, 0].rearrange("(t p) c -> p t c", p=P))
        normed = self.norm_to_xT(self.h_tile, two, D, f"ple{layer}", self.xT, self.V.now())
        self.turn(lambda t, rows, k: p_tm[:, t, k * P:(k + 1) * P], two, 2, pT, p_loaded)
        gate = self.proj[:, 0:2048].rearrange("p (t c) -> p t c", t=NT)
        self.linear(N_OUT, two, self.to(gate, ACT.Sigmoid), normed)
        tmp = self.work[:, 4096:6144].rearrange("p (n t w) -> p n t w", n=4, t=NT)

        def evac(n, products):
            got = self.ps[:, n, :].rearrange("p (t w) -> p t w", t=NT)
            cols = slice(n * CW, (n + 1) * CW)
            self.v(lambda e: e.tensor_tensor(tmp[:, n], got, gate[:, :, cols], ALU.mult), products)
            return self.v(lambda e: e.tensor_tensor(self.h[:, 0:NT, cols], self.h[:, 0:NT, cols], tmp[:, n], ALU.add))
        return self.product(2, D, two, pT, evac)

    def spatial(self, z):
        T, V, w = self.T, self.V, self.work
        self.fence()
        wsT = w[:, 0:1024].rearrange("p (g t) -> p g t", g=8)
        loaded = self.load(w[:, 0:1024], self.a["spatial"])
        sm = self.small
        mu, var, r, tmp = sm[:, 0:2], sm[:, 4:6], sm[:, 8:10], sm[:, 12:14]
        vv = z[:, :, D:2 * D]
        scr = w[:, 2048:4096].rearrange("p (t c) -> p t c", t=NT)
        self.v(lambda e: e.tensor_reduce(mu, vv, AX_X, ALU.add))
        self.v(lambda e: e.tensor_scalar(mu, mu, 1.0 / D, None, ALU.mult))
        self.v(lambda e: e.tensor_tensor(vv, vv, mu.unsqueeze(2).to_broadcast([P, NT, D]), ALU.subtract))
        self.v(lambda e: e.tensor_tensor(scr, vv, vv, ALU.mult))
        self.v(lambda e: e.tensor_reduce(var, scr, AX_X, ALU.add))
        ready = self.v(lambda e: e.tensor_scalar(var, var, 1.0 / D, 1e-5, ALU.mult, ALU.add))
        self.rsqrt(r, var, tmp, ready)
        for t in range(NT):
            self.v(lambda e: e.scalar_tensor_tensor(vv[:, t, :], vv[:, t, :], r[:, t:t + 1], self.row("lng"),
                                                    ALU.mult, ALU.mult))
            normed = self.v(lambda e: e.tensor_tensor(vv[:, t, :], vv[:, t, :], self.row("lnb"), ALU.add))
        tril = self.const("tril").unsqueeze(1).to_broadcast([P, 8, P])
        masked = self.v(lambda e: e.tensor_tensor(wsT, wsT, tril, ALU.mult), loaded)
        T.wait(masked)
        for g in range(8):
            ins = T.e.matmul(self.ps[:, g, 0:SEQ], wsT[:, g, :], vv[:, :, g * P:(g + 1) * P], start=True, stop=True)
            made = T.did(ins)
            V.wait(made)
            cols = slice(g * P, (g + 1) * P)
            done = V.did(V.e.scalar_tensor_tensor(self.mix[:, :, cols], self.ps[:, g, 0:SEQ].rearrange(
                "p (t c) -> p t c", t=NT), self.col("bs", g), z[:, :, cols], ALU.add, ALU.mult))
        return done

    def route(self, normed):
        T, A, V, w = self.T, self.A, self.V, self.work
        self.fence()
        rw = w[:, 4096:4160].rearrange("p (k e) -> p k e", k=KT)
        lg = w[:, 4160:4176].rearrange("p (t e) -> p t e", t=NT)
        top = w[:, 4176:4192].rearrange("p (t e) -> p t e", t=NT)
        idx = w[:, 4192:4208].bitcast(U32).rearrange("p (t e) -> p t e", t=NT)
        idf = w[:, 4208:4224].rearrange("p (t e) -> p t e", t=NT)
        pick = w[:, 4224:4256].rearrange("p (t c e) -> p t c e", t=NT, c=2)
        gate = w[:, 4256:4272].rearrange("p (t e) -> p t e", t=NT)
        sm = self.small
        wide = w[:, 4352:4352 + NT * NEXP * FG].rearrange("p (t e g) -> p t e g", t=NT, e=NEXP)
        loaded = self.load(rw, self.a["router_w_2"][0].rearrange("(k p) e -> p k e", p=P))
        T.wait(loaded, normed)
        for t in range(NT):
            for k in range(KT):
                ins = T.e.matmul(self.ps[:, 4, t * 8:(t + 1) * 8], self.xT[:, k, t * P:(t + 1) * P], rw[:, k, :],
                                 start=(k == 0), stop=(k == KT - 1))
        made = T.did(ins)
        self.v(lambda e: e.tensor_copy(lg, self.ps[:, 4, 0:16].rearrange("p (t e) -> p t e", t=NT)), made)
        for t in range(NT):
            self.v(lambda e: e.max(top[:, t, :], lg[:, t, :]))
            self.v(lambda e: e.max_index(idx[:, t, :], top[:, t, :], lg[:, t, :]))
        self.v(lambda e: e.tensor_copy(idf, idx))
        d, e1, r = sm[:, 210:212], sm[:, 212:214], sm[:, 214:216]
        diff = self.v(lambda e: e.tensor_tensor(d, top[:, :, 1], top[:, :, 0], ALU.subtract))
        ex = self.s(lambda e: e.activation(e1, d, ACT.Exp), diff)
        self.v(lambda e: e.tensor_scalar(r, e1, 1.0, None, ALU.add), ex)
        self.v(lambda e: e.reciprocal(r, r))
        self.v(lambda e: e.tensor_tensor(e1, e1, r, ALU.mult))
        for t in range(NT):
            self.v(lambda e: e.tensor_scalar(gate[:, t, :], self.const("experts"), idf[:, t, 0:1], r[:, t:t + 1],
                                             ALU.is_equal, ALU.mult))
            self.v(lambda e: e.tensor_scalar(pick[:, t, 0, :], self.const("experts"), idf[:, t, 1:2], e1[:, t:t + 1],
                                             ALU.is_equal, ALU.mult))
            self.v(lambda e: e.tensor_tensor(gate[:, t, :], gate[:, t, :], pick[:, t, 0, :], ALU.add))
            done = self.v(lambda e: e.tensor_copy(wide[:, t], gate[:, t, :].unsqueeze(2).to_broadcast([P, NEXP, FG])))
        return w[:, 4352:4352 + NT * NEXP * FG].rearrange("p (t g) -> p t g", t=NT), done

    def block2(self, ready):
        two = [P] * NT
        self.fence()
        normed = self.norm_to_xT(self.h_tile, two, D, "mix0", self.xT, ready)
        pr = self.proj[:, 0:2 * 3072].rearrange("p (t c) -> p t c", t=NT)
        self.linear(N_IN2, two, self.to(pr), normed)
        attended = self.diff_attention(pr)
        self.mix_to_xT(attended, 4)
        conved = self.conv(pr)
        added = self.linear(N_OUT, two, self.add_to_h(), conved)
        self.fence()
        normed = self.norm_to_xT(self.h_tile, two, D, "ffn0", self.xT, added)
        self.swiglu(FG, normed)
        self.ple(0)
        self.fence()
        normed = self.norm_to_xT(self.h_tile, two, D, "mix1", self.xT, self.V.now())
        z = self.proj[:, 0:2 * 2048].rearrange("p (t c) -> p t c", t=NT)
        self.linear(N_CIN, two, self.to(z, ACT.Gelu), normed)
        gated = self.spatial(z)
        added = self.linear(N_OUT, two, self.add_to_h(), self.mix_to_xT(gated))
        self.fence()
        normed = self.norm_to_xT(self.h_tile, two, D, "ffn1", self.xT, added)
        gates, routed = self.route(normed)
        self.swiglu(NEXP * FG, routed, gates)
        self.ple(1)
        self.fence()
        return self.final_norm("final2", self.V.now())

    def rope3(self, x, heads, half, rows, t, name, scratch):
        cos = self.const(f"cos{half}").rearrange("p (t f) -> p t f", t=NT + 1)[0:rows, t]
        sin = self.const(f"sin{half}").rearrange("p (t f) -> p t f", t=NT + 1)[0:rows, t]
        cb = cos.unsqueeze(1).to_broadcast([rows, heads, half])
        sb = sin.unsqueeze(1).to_broadcast([rows, heads, half])
        return self.rope(x[:, :, 0:half], x[:, :, half:2 * half], cb, sb, (heads, half), scratch, None)

    def key_columns(self, dst, sources):
        return ([(sources(NT)[0:META], META)] + [(sources(t), P) for t in range(NT)], dst)

    def block3(self, ready):
        T, A, V, w = self.T, self.A, self.V, self.work
        two, three = [P] * NT, [P] * NT + [META]
        self.fence()
        normed = self.norm_to_xT(self.h_tile, three, D, "attn3", self.xT, ready)
        pr = self.proj[:, :].rearrange("p (t c) -> p t c", t=NT + 1)
        self.with_meta = True
        self.linear(N_IN3, three, self.to(pr), normed)
        self.with_meta = False
        self.fence()
        blocks = [(0, META), (META, P), (META + P, P)]
        tile_of = (NT, 0, 1)
        cqT = w[:, 0:512].rearrange("p (k s) -> p k s", k=2)
        ckvT = w[:, 512:512 + KEYS3].rearrange("p (k s) -> p k s", k=1)
        kv = w[:, 784:784 + 3072].rearrange("p (t c) -> p t c", t=3)
        qT = w[:, 3856:5904].rearrange("p (h s) -> p h s", h=8)
        kT = w[:, 5904:8080].rearrange("p (h s) -> p h s", h=8)
        q = self.xT[:, :, :].rearrange("p k s -> p (k s)")[:, 0:1536].rearrange("p (t c) -> p t c", t=NT)
        self.norm_small(pr, 0, 256, two, "q3", cqT)
        self.norm_small(pr, 256, P, three, "kv3", ckvT)

        def to_q(n, products):
            cols = slice(n * CW, (n + 1) * CW)
            return self.s(lambda e: e.copy(q[:, :, cols], self.ps[:, n, :].rearrange("p (t w) -> p t w", t=NT)),
                          products)

        def to_kv(n, products):
            cols = slice(n * CW, (n + 1) * CW)
            self.s(lambda e: e.copy(kv[:, 0:NT, cols], self.ps[:, n, :].rearrange("p (t w) -> p t w", t=NT)),
                   products)
            return self.s(lambda e: e.copy(kv[0:META, NT, cols], self.ps[0:META, 4 + n, 0:CW]))
        self.product(2, 768, two, cqT, to_q)
        self.product(1, D, three, ckvT, to_kv)
        self.fence()
        scratch = self.mix[:, :, :].rearrange("p t d -> p (t d)")
        for t in range(NT):
            self.rope3(q[:, t, :].rearrange("p (h d) -> p h d", h=8)[:, :, 64:96], 8, 16, P, t, "q", scratch)
        for t, rows in enumerate(three):
            self.rope3(pr[0:rows, t, 384:416].unsqueeze(1), 1, 16, rows, t, "kr", scratch)
            self.rope3(pr[0:rows, t, 928:1440].rearrange("p (h d) -> p h d", h=8), 8, 32, rows, t, "ks", scratch)
            self.rope3(pr[0:rows, t, 2464:2528].unsqueeze(1), 1, 32, rows, t, "ki", scratch)
            if rows == P:
                self.rope3(pr[0:rows, t, 416:928].rearrange("p (h d) -> p h d", h=8), 8, 32, rows, t, "qs", scratch)
                self.rope3(pr[0:rows, t, 1952:2464].rearrange("p (h d) -> p h d", h=8), 8, 32, rows, t, "qi", scratch)
        self.fence()
        jobs = []
        for h in range(0, 8, 2):
            jobs.append(([(q[:, t, (h + u) * 96:(h + u + 1) * 96], P) for u in range(2) for t in range(NT)],
                         qT[0:96, h:h + 2, :].rearrange("p h s -> p (h s)")))
        for h in range(8):
            jobs.append(self.key_columns(kT[0:64, h, :], lambda t: kv[:, t, h * P:h * P + 64]))
        self.turn_heads(jobs, ())
        T.wait(A.now(), V.now())
        at = 0
        for t, rows in ((NT, META), (0, P), (1, P)):
            ins = T.e.transpose(self.ps[0:32, 4, at:at + rows], pr[0:rows, t, 384:416], self.const("ident")[0:rows, 0:rows])
            at += rows
        turned = T.did(ins)
        self.s(lambda e: e.copy(kT[64:96, :, :], self.ps[0:32, 4, 0:KEYS3].unsqueeze(1).to_broadcast([32, 8, KEYS3])),
               turned)
        causal = self.const("causal3").rearrange("p (t k) -> p t k", t=NT)
        self.attend(8, 96, KEYS3, lambda h, t: qT[0:96, h, t * P:(t + 1) * P], lambda h: kT[0:96, h, :],
                    lambda h, b: kv[0:blocks[b][1], tile_of[b], h * P + 64:(h + 1) * P],
                    blocks, 96 ** -0.5, lambda h: causal, lambda h: self.mix[:, :, h * 64:(h + 1) * 64], 64,
                    (A.now(), V.now()))
        self.fence()
        kiT = w[:, 0:KEYS3]
        score = w[:, 272:816].rearrange("p (t k) -> p t k", t=NT)
        keep = w[:, 816:1360].rearrange("p (t k) -> p t k", t=NT)
        relu = w[:, 1360:1904].rearrange("p (t k) -> p t k", t=NT)
        qiT = w[:, 1904:3952].rearrange("p (h s) -> p h s", h=8)
        qsT = w[:, 3952:6000].rearrange("p (h s) -> p h s", h=8)
        ksT = w[:, 6000:8176].rearrange("p (h s) -> p h s", h=8)
        jobs = [self.key_columns(kiT[0:64, :], lambda t: pr[:, t, 2464:2528])]
        for base, dst in ((1952, qiT), (416, qsT)):
            for h in range(0, 8, 2):
                jobs.append(([(pr[:, t, base + (h + u) * 64:base + (h + u + 1) * 64], P) for u in range(2)
                              for t in range(NT)], dst[0:64, h:h + 2, :].rearrange("p h s -> p (h s)")))
        for h in range(8):
            jobs.append(self.key_columns(ksT[0:64, h, :], lambda t: pr[:, t, 928 + h * 64:928 + (h + 1) * 64]))
        self.turn_heads(jobs, ())
        self.index_scores(pr, qiT, kiT, score, relu)
        self.choose(score, relu, keep, causal)
        self.attend(8, 64, KEYS3, lambda h, t: qsT[0:64, h, t * P:(t + 1) * P], lambda h: ksT[0:64, h, :],
                    lambda h, b: pr[0:blocks[b][1], tile_of[b], 1440 + h * 64:1440 + (h + 1) * 64],
                    blocks, 64 ** -0.5, lambda h: keep, lambda h: self.mix[:, :, 512 + h * 64:512 + (h + 1) * 64], 64,
                    (A.now(), V.now()))
        self.fence()
        added = self.linear(N_OUT, two, self.add_to_h(), self.mix_to_xT(self.V.now()))
        self.fence()
        normed = self.norm_to_xT(self.h_tile, two, D, "ffn3", self.xT, added)
        self.swiglu(FG, normed)
        self.fence()
        return self.final_norm("final3", self.V.now())

    def norm_small(self, pr, lo, width, tiles, gain, dst):
        r = self.rms_scale(lambda t, rows: pr[0:rows, t, lo:lo + width], tiles, width, None)
        hn = self.mix[:, :, :].rearrange("p t d -> p (t d)")[:, 0:768].rearrange("p (t c) -> p t c", t=3)
        for t, rows in enumerate(tiles):
            normed = self.v(lambda e: e.tensor_scalar(hn[0:rows, t, 0:width], pr[0:rows, t, lo:lo + width],
                                                      r[0:rows, t:t + 1], None, ALU.mult))
        self.turn(lambda t, rows, k: hn[0:rows, t, k * P:(k + 1) * P], tiles, width // P, dst, normed, gain)
        self.fence()

    def index_scores(self, pr, qiT, kiT, score, relu):
        T, A, V, ps = self.T, self.A, self.V, self.ps
        self.fence()
        wi = self.small[:, 64:80].rearrange("p (t h) -> p t h", t=NT)
        self.v(lambda e: e.tensor_scalar(wi, pr[:, 0:NT, 2528:2536], 8 ** -0.5, None, ALU.mult))
        self.v(lambda e: e.memset(score, 0.0))
        for h in range(8):
            T.wait(A.now())
            for t in range(NT):
                ins = T.e.matmul(ps[:, 2 * (h % 2) + t, 0:KEYS3], qiT[0:64, h, t * P:(t + 1) * P], kiT[0:64, :],
                                 start=True, stop=True)
            made = T.did(ins)
            pos = self.s(lambda e: e.activation(relu, ps[:, 2 * (h % 2):2 * (h % 2) + 2, 0:KEYS3], ACT.Relu,
                                                scale=64 ** -0.5), made, V.now())
            for t in range(NT):
                self.v(lambda e: e.scalar_tensor_tensor(score[:, t, :], relu[:, t, :], wi[:, t, h:h + 1],
                                                        score[:, t, :], ALU.mult, ALU.add), pos)

    def choose(self, score, left, keep, causal):
        best = self.small[:, 80:96].rearrange("p (t e) -> p t e", t=NT)
        self.v(lambda e: e.tensor_tensor(left, score, causal, ALU.add))
        for _ in range(TOPK3 // 8):
            for t in range(NT):
                self.v(lambda e: e.max(best[:, t, :], left[:, t, :]))
                self.v(lambda e: e.match_replace(left[:, t, :], best[:, t, :], left[:, t, :], TAKEN))
        self.v(lambda e: e.tensor_scalar(keep, left, TAKEN, None, ALU.is_equal))
        self.v(lambda e: e.tensor_scalar(keep, keep, -NEG, NEG, ALU.mult, ALU.add))
        self.v(lambda e: e.tensor_tensor(keep, keep, causal, ALU.add))
        self.fence()


def three_blocks(nc, args, out, plan, blocks=(1, 2, 3)):
    c = Core(nc, plan)
    m = Model(c, args)
    m.u = nc.dram_tensor("bias_vectors", [2, 8, 512], F32).ap()
    stream_weights(c, args["stream"], m.ring)
    ready = m.set_up()
    lanes = (c.T, c.A, c.V)
    for lane in lanes:
        lane.wait(ready)
    m.bias_vectors(ready)
    m.fence()
    if 1 in blocks:
        ready = m.block1(ready)
    if 2 in blocks:
        ready = m.block2(ready)
    if 3 in blocks:
        ready = m.block3(ready)
    c.A.wait(ready)
    s_out = nc.alloc_semaphore("out_stored")
    c.A.e.dma_start(out.rearrange("b (t p) d -> p (b t) d", p=P), m.h[:, 0:NT, :]).then_inc(s_out, 16)
    c.A.e.wait_ge(s_out, 16)
    assert c.chunk == args["stream"].shape[0], (c.chunk, args["stream"].shape[0])



def shape_constants():
    import math
    import numpy as np
    i = np.arange(P)
    k = np.zeros((P, N_CONST), np.float32)

    def put(name, value):
        at, width = CONSTS[name]
        k[:, at:at + width] = value.reshape(P, width)

    put("ident", np.eye(P))
    put("flip", np.eye(P)[::-1])
    same = i[:, None] // 64 == i[None, :] // 64
    put("tri", same & (i[:, None] <= i[None, :]))
    put("same", same)
    put("half", i[:, None] // 64 == np.arange(2)[None, :])
    put("tril", i[:, None] <= i[None, :])
    q = i[:, None, None] + P * np.arange(NT)[None, :, None]
    put("causal", np.where(np.arange(SEQ)[None, None, :] <= q, 0.0, NEG))
    put("causal3", np.where(np.arange(KEYS3)[None, None, :] <= q + META, 0.0, NEG))
    pos = np.concatenate([META + np.arange(SEQ), np.arange(P)]).astype(np.float32).reshape(NT + 1, P).T
    for half in (16, 32):
        inv = np.power(np.float32(10000.0), -np.arange(half, dtype=np.float32) / np.float32(half))
        ang = (pos[:, :, None] * inv[None, None, :]).astype(np.float64)
        put(f"cos{half}", np.cos(ang))
        put(f"sin{half}", np.sin(ang))
    put("experts", np.broadcast_to(np.arange(NEXP), (P, NEXP)))
    m = np.arange(512)
    dist = 255 - m
    n = np.maximum(dist, 0)
    large = 16 + (np.log(np.maximum(n, 1).astype(np.float32) / 16) / math.log(8) * 16).astype(np.int32)
    bucket = np.where(n < 16, n, np.minimum(large, 31))
    hot = np.zeros((33, 2, 512), np.float32)
    for kind, window in enumerate((256, 128)):
        seen = (dist >= 0) & (dist < window)
        hot[bucket[seen], kind, m[seen]] = 1.0
        hot[32, kind, ~seen] = 1.0
    return k, hot.reshape(33, 1024)


def weight_stream(w):
    import numpy as np

    def wide(a):
        n = -(-a.shape[1] // CW)
        full = np.zeros((D, n * CW), a.dtype)
        full[:, :a.shape[1]] = a
        return full.reshape(KT, P, n, CW).transpose(2, 1, 0, 3).reshape(n, P, CHUNK)

    def tall(a):
        k = a.shape[0] // P
        full = np.zeros((P, CHUNK), a.dtype)
        full[:, :k * a.shape[1]] = a.reshape(k, P, -1).transpose(1, 0, 2).reshape(P, -1)
        return full[None]

    def swiglu(w1, w3, w2):
        e = w1.shape[0]
        up = np.empty((e, FF // P, P, KT, 2, P), w1.dtype)
        up[:, :, :, :, 0] = w1.reshape(e, KT, P, FF // P, P).transpose(0, 3, 2, 1, 4)
        up[:, :, :, :, 1] = w3.reshape(e, KT, P, FF // P, P).transpose(0, 3, 2, 1, 4)
        up = up.reshape(e * FG, 2, P, CHUNK)
        down = w2.reshape(e * FG, 2, P, D).transpose(0, 2, 1, 3).reshape(e * FG, P, CHUNK)
        full = np.empty((e * FG, 3, P, CHUNK), w1.dtype)
        full = full.reshape(-1, P, CHUNK)
        full[0:2] = up[0]
        body = full[2:-1].reshape(e * FG - 1, 3, P, CHUNK)
        body[:, 0:2] = up[1:]
        body[:, 2] = down[:-1]
        full[-1] = down[-1]
        return full

    e = w["w_in_even"][0]
    e = np.concatenate([e[:, 0:1024], e[:, 1040:2832], e[:, 1024:1040]], axis=1)
    parts = [
        wide(e), wide(w["w_out_even"][0]), wide(w["w_in_odd"][0]), wide(w["w_out_odd"][0]),
        wide(w["a_w_in_2"][0]), wide(w["a_w_out_2"][0]), swiglu(w["ffn_w1_2"], w["ffn_w3_2"], w["ffn_w2_2"]),
        wide(w["ple_gate_2"][0]), tall(w["ple_proj_2"][0]), wide(w["c_w_in_2"][0]), wide(w["c_w_out_2"][0]),
        swiglu(w["moe_w1_2"][0], w["moe_w3_2"][0], w["moe_w2_2"][0]),
        wide(w["ple_gate_2"][1]), tall(w["ple_proj_2"][1]),
        wide(w["w_in_3"][0]), tall(w["w_uq_3"][0]), tall(w["w_ukv_3"][0]), wide(w["w_o_3"][0]),
        swiglu(w["w_gate_3"], w["w_up_3"], w["w_down_3"]),
    ]
    cuts = (0, 4, 14, len(parts))
    return parts, cuts


def small_arrays(w):
    import numpy as np
    cols = np.zeros((P, N_COLS), np.float32)

    def put(name, a, width):
        at = COLS[name][0]
        cols[:, at:at + width] = a.reshape(width, P).T

    for name, a in (("norm0", w["norm_gain"][0]), ("norm1", w["norm_gain"][1]), ("mix0", w["ln_mix_2"][0]),
                    ("mix1", w["ln_mix_2"][1]), ("ffn0", w["ln_ffn_2"][0]), ("ffn1", w["ln_ffn_2"][1]),
                    ("ple0", w["ln_ple_2"][0]), ("ple1", w["ln_ple_2"][1]), ("attn3", w["attn_norm_g_3"][0]),
                    ("ffn3", w["ffn_norm_g_3"][0]), ("q3", w["mla_q_norm_g_3"][0]),
                    ("kv3", w["mla_kv_norm_g_3"][0]), ("bs", w["c_b_s_2"][0]),
                    ("conv", np.ascontiguousarray(w["a_conv_w_2"][0].T))):
        put(name, a, COLS[name][1])
    freq = np.float32(500000.0) ** (-np.arange(0, 16, 2, dtype=np.float32) / np.float32(16))
    rows = np.concatenate([w["final_gain"], w["c_ln_g_2"][0], w["c_ln_b_2"][0], w["final_norm_2"],
                           w["final_norm_g_3"], w["gla_norm_gain"][0], w["a_subln_2"][0], w["swa_sinks"][0],
                           w["a_lambda_2"][0].reshape(-1), freq.astype(np.float32)])[None]
    up = np.concatenate([w["gla_w_up"][0], w["gla_b_up"][0][None]], axis=0)
    spatial = w["c_w_s_2"][0].transpose(2, 0, 1).reshape(P, 8 * P)
    return {"cols": cols, "rows": rows, "gla_up": up, "spatial": spatial}


def build(nc_of, arrays, blocks=(1, 2, 3)):
    plan = {}
    for _ in range(2):
        nc = nc_of()
        args = {name: nc.dram_tensor(f"in_{name}", a.shape, mybir.dt.from_np(a.dtype), kind="ExternalInput").ap()
                for name, a in arrays.items()}
        out = nc.dram_tensor("out_0", (1, SEQ, D), F32, kind="ExternalOutput").ap()
        three_blocks(nc, args, out, plan, blocks)
    return nc


def host_arrays(inputs, blocks=(1, 2, 3)):
    import numpy as np
    w = {name: np.asarray(a) for name, a in inputs.items()}
    parts, cuts = weight_stream(w)
    parts = [p for b in blocks for p in parts[cuts[b - 1]:cuts[b]]]
    consts, buckets = shape_constants()
    arrays = {"stream": np.concatenate(parts), "consts": consts, "buckets": buckets, **small_arrays(w)}
    arrays["positions"] = w["positions_2"].reshape(NT, P).T
    for name in ("x", "rel_bias", "p_2", "router_w_2", "meta_tokens_3"):
        arrays[name] = np.ascontiguousarray(w[name])
    return {name: np.ascontiguousarray(a) for name, a in arrays.items()}


def kernel(**inputs):
    import concourse.bacc as bacc
    from concourse.bass_utils import run_bass_kernel_spmd

    arrays = host_arrays(inputs)
    nc = build(lambda: bacc.Bacc("TRN2", target_bir_lowering=False, num_devices=1), arrays)
    result = run_bass_kernel_spmd(nc, [{f"in_{name}": a for name, a in arrays.items()}], core_ids=[0])
    return result.results[0]["out_0"]
```

```python
from contextlib import contextmanager

import concourse.bass as bass
from concourse import mybir

F32 = mybir.dt.float32
F32R = mybir.dt.float32r
I32 = mybir.dt.int32
U32 = mybir.dt.uint32
ALU = mybir.AluOpType
ACT = mybir.ActivationFunctionType
AX_X = mybir.AxisListType.X
ENG = mybir.EngineType
ds = bass.ds

P = 128
D = 1024
KT = D // P
SEQ = 256
NT = SEQ // P
META = 16
KEYS3 = META + SEQ
CHUNK = 2048
CW = CHUNK // KT
RING = 3
HALF = CHUNK // 2
PARTS = 3
AHEAD = 2
FF = 2816
FG = FF // (2 * P)
NEXP = 8
TOPK3 = 64
NEG = -1.0e30
SLOTS = 128
TAKEN = -3.0e38
PI = 3.141592653589793

N_IN1, N_OUT, N_ODD, N_IN2, N_CIN, N_IN3 = 12, 4, 10, 12, 8, 10
FFN_CHUNKS = 3 * FG

WORK = 9216
SWI = 0
MOE = 3328
SCR = WORK - D
CONSTS = {}
_at = 0
for _name, _width in (("ident", P), ("flip", P), ("tri", P), ("same", P), ("half", 2), ("tril", P),
                      ("causal", NT * SEQ), ("causal3", NT * KEYS3), ("cos16", 48), ("sin16", 48),
                      ("cos32", 96), ("sin32", 96), ("experts", NEXP), ("upto", P), ("slots", SLOTS)):
    CONSTS[_name] = (_at, _width)
    _at += _width
N_CONST = _at

COLS = {}
_at = 0
for _name, _width in (("norm0", 8), ("norm1", 8), ("mix0", 8), ("mix1", 8), ("ffn0", 8), ("ffn1", 8),
                      ("ple0", 8), ("ple1", 8), ("attn3", 8), ("ffn3", 8), ("q3", 2), ("kv3", 1),
                      ("conv", 12), ("bs", 8)):
    COLS[_name] = (_at, _width)
    _at += _width
N_COLS = _at

ROWS = {}
_at = 0
for _name, _width in (("gla", P), ("subln", P), ("sinks", 8), ("lambda", 256), ("freq", 8)):
    ROWS[_name] = (_at, _width)
    _at += _width
N_ROWS = _at
WIDE_ROWS = ("final1", "lng", "lnb", "final2", "final3")


class Lane:

    def __init__(self, name, eng, sem):
        self.name, self.e, self.sem = name, eng, sem
        self.n = 0
        self.turn = 0
        self.seen = {}

    def now(self):
        return (self.sem, self.turn + self.n if self.n else 0)

    def did(self, ins):
        ins.then_inc(self.sem, 1)
        self.n += 1
        return self.now()

    def wait(self, *tokens):
        for token in tokens:
            if token is None:
                continue
            sem, value = token
            if type(value) is int:
                if value <= self.seen.get(sem.num, 0):
                    continue
                self.seen[sem.num] = value
            self.e.wait_ge(sem, value)


class Flow:

    def __init__(self, nc, name):
        self.landed = [[nc.alloc_semaphore(f"{name}_landed{k}_{half}") for half in range(2)] for k in range(RING)]
        self.high_made = nc.alloc_semaphore(f"{name}_high_made")
        self.split = nc.alloc_semaphore(f"{name}_split")
        self.used = nc.alloc_semaphore(f"{name}_used")


class At:

    def __init__(self, n, turns=0):
        self.n, self.turns = n, turns

    def __add__(self, k):
        return At(self.n + k, self.turns)

    def count(self, more=0):
        return self.turns * PARTS + (self.n + more)

    def halves(self, more=0):
        return self.turns * (2 * PARTS) + (2 * self.n + more)


class Core:

    def __init__(self, nc, plan):
        self.nc, self.plan = nc, plan
        self.T = Lane("pe", nc.tensor, nc.alloc_semaphore("pe_steps"))
        self.A = Lane("act", nc.scalar, nc.alloc_semaphore("act_steps"))
        self.V = Lane("dve", nc.vector, nc.alloc_semaphore("dve_steps"))
        self.G = Lane("pool", nc.gpsimd, nc.alloc_semaphore("pool_steps"))
        self.flow = Flow(nc, "chunk")
        self.chunk = 0
        self.loops = 0

    def buf(self, name, shape, dtype=F32):
        return self.nc.alloc_sbuf_tensor(name, shape, dtype)

    @contextmanager
    def loop(self, n, lanes):
        self.loops += 1
        me = self.loops
        start = {lane.name: lane.n for lane in lanes}
        per = {lane.name: self.plan.get((me, lane.name), 0) for lane in lanes}
        kind = {"pe": ENG.PE, "act": ENG.Activation, "dve": ENG.DVE, "pool": ENG.Pool}
        with self.nc.Fori(0, n, engines=tuple(kind[lane.name] for lane in lanes)) as i:
            before = {lane.name: lane.turn for lane in lanes}
            for lane in lanes:
                lane.turn = lane.turn + i * per[lane.name]

            def label(name, lane):
                self.plan[me, name] = (lane.n - start[lane.name],)

            def prev(name, lane):
                offset = self.plan.get((me, name), (0,))[0]
                return (lane.sem, lane.turn + (start[lane.name] + offset - per[lane.name]))

            yield i, label, prev
            for lane in lanes:
                steps = lane.n - start[lane.name]
                self.plan[me, lane.name] = steps
                lane.turn = before[lane.name]
                lane.n = start[lane.name] + n * steps


def stream_weights(c, flow, stream, ring, lo, hi):
    sp = c.nc.sync

    def load(k, turn):
        for half in range(2):
            if type(turn) is not int or k >= RING:
                sp.wait_ge(flow.split, turn * (2 * RING) + (2 * (k - RING) + half + 1))
            cols = slice(half * HALF, (half + 1) * HALF)
            sp.dma_start(ring[:, k % RING, cols], stream[turn * RING + (k + lo), :, cols]).then_inc(
                flow.landed[k % RING][half], 16)
    return load


def stream_part(c, flow, stream, ring, first, last, offset):
    load = stream_weights(c, flow, stream, ring, offset, last)
    k, end = first - offset, last - offset
    while k < end and (k < RING or k % RING):
        load(k, 0)
        k += 1
    turns = (end - k) // RING
    if turns > 1:
        with c.nc.Fori(0, turns, engines=(ENG.SP,)) as r:
            for j in range(RING):
                load(k + j, r)
        k += turns * RING
    for k in range(k, end):
        load(k, 0)


class Model:
    def __init__(self, c, args):
        nc = c.nc
        self.c, self.a = c, args
        self.T, self.A, self.V, self.G = c.T, c.A, c.V, c.G
        self.ring = c.buf("ring", [P, RING, CHUNK])
        self.high = c.buf("high", [P, PARTS, CHUNK], F32R)
        self.low = c.buf("low", [P, PARTS, CHUNK], F32R)
        self.consts = c.buf("consts", [P, N_CONST])
        self.cols = c.buf("cols", [P, N_COLS])
        self.rows = c.buf("rows", [P, N_ROWS])
        self.wide = c.buf("wide", [P, 2, D])
        self.h = c.buf("h", [P, NT, D])
        self.xT = (c.buf("xT_high", [P, KT, KEYS3], F32R), c.buf("xT_low", [P, KT, KEYS3], F32R))
        self.smallT = (c.buf("smallT_high", [P, 512], F32R), c.buf("smallT_low", [P, 512], F32R))
        self.proj = c.buf("proj", [P, 8192])
        self.mix = c.buf("mix", [P, NT, D])
        self.work = c.buf("work", [P, WORK])
        self.logit = c.buf("logit", [P, 2, NT, KEYS3])
        self.probT = c.buf("probT", [P, 2, NT * NT, P])
        self.probM = c.buf("probM", [META, 2, NT, P])
        self.small = c.buf("small", [P, 256])
        self.ps = nc.alloc_psum_tensor("ps", [P, 8, 512], F32)
        self.s_param = nc.alloc_semaphore("params_landed")
        self.params = 0
        self.unsplit = 0

    def const(self, name, rows=P):
        at, width = CONSTS[name]
        return self.consts[0:rows, at:at + width]

    def col(self, name, k):
        at, _ = COLS[name]
        return self.cols[:, at + k:at + k + 1]

    def row(self, name):
        at, width = ROWS[name]
        return self.rows[:, at:at + width]

    def load(self, dst, src):
        self.A.e.dma_start(dst, src).then_inc(self.s_param, 16)
        self.params += 1
        return (self.s_param, 16 * self.params)

    def fence(self):
        lanes = (self.T, self.A, self.V)
        marks = [lane.now() for lane in lanes if lane.n]
        if self.c.chunk:
            marks.append((self.c.flow.used, self.c.chunk))
        for lane in lanes:
            lane.wait(*marks)

    def fence_steps(self):
        for lane in (self.T, self.A, self.V):
            lane.wait(self.T.now(), self.A.now(), self.V.now(), (self.c.flow.used, self.c.chunk - AHEAD))

    def v(self, make, *after):
        self.V.wait(self.V.now() if self.V.n else None, *after)
        return self.V.did(make(self.V.e))

    def s(self, make, *after):
        self.A.wait(self.A.now() if self.A.n else None, *after)
        return self.A.did(make(self.A.e))

    def rsqrt(self, out, var, scratch, ready):
        root = self.s(lambda e: e.activation(out, var, ACT.Sqrt), ready)
        self.v(lambda e: e.reciprocal(out, out), root)
        self.v(lambda e: e.tensor_tensor(scratch, out, out, ALU.mult))
        self.v(lambda e: e.tensor_tensor(scratch, scratch, var, ALU.mult))
        self.v(lambda e: e.tensor_scalar(scratch, scratch, -0.5, 1.5, ALU.mult, ALU.add))
        return self.v(lambda e: e.tensor_tensor(out, out, scratch, ALU.mult))

    def rms_scale(self, src, tiles, width, ready, eps=1e-6):
        ss, r, tmp = self.small[:, 0:3], self.small[:, 4:7], self.small[:, 8:11]
        scratch = self.work[:, SCR:SCR + D]
        if any(rows < P for rows in tiles):
            self.v(lambda e: e.memset(ss, 1.0), ready)
        for t, rows in enumerate(tiles):
            scr = scratch[0:rows, 0:width]
            done = self.s(lambda e: e.activation(scr, src(t, rows), ACT.Square,
                                                 accum_out=ss[0:rows, t:t + 1]), ready, self.V.now())
        n = len(tiles)
        done = self.v(lambda e: e.tensor_scalar(ss[:, 0:n], ss[:, 0:n], 1.0 / width, eps, ALU.mult, ALU.add), done)
        self.rsqrt(r[:, 0:n], ss[:, 0:n], tmp[:, 0:n], done)
        return r

    def turn(self, src, tiles, k_tiles, dst, ready, gain=None):
        T, A, V = self.T, self.A, self.V
        ident = self.const("ident")
        freed = [None] * 4
        T.wait(ready, A.now(), V.now())
        width = sum(tiles)
        step = 2 if width <= 256 else 1
        for b, k0 in enumerate(range(0, k_tiles, step)):
            ks = list(range(k0, min(k0 + step, k_tiles)))
            bank = b % 4
            T.wait(freed[bank])
            for n, k in enumerate(ks):
                at = 0
                for t, rows in enumerate(tiles):
                    ins = T.e.transpose(self.ps[0:P, bank, n * width + at:n * width + at + rows],
                                        src(t, rows, k), ident[0:rows, 0:rows])
                    at += rows
            turned = T.did(ins)
            A.wait(turned, ready)
            if type(dst) is not tuple:
                got = self.ps[:, bank, 0:len(ks) * width].rearrange("p (k w) -> p k w", w=width)
                done = A.did(A.e.copy(dst[:, k0:k0 + len(ks), 0:width], got))
            else:
                done = self.to_parts(dst, [(k, self.ps[:, bank, n * width:(n + 1) * width], gain)
                                           for n, k in enumerate(ks)], width)
            freed[bank] = done
        return done

    def to_parts(self, dst, items, width):
        A, V = self.A, self.V
        high, low = dst
        for k, src, gain in items:
            g = 1.0 if gain is None else self.col(gain, k)
            made = A.did(A.e.activation(high[:, k, 0:width], src, ACT.Copy, scale=g))
        V.wait(made)
        for k, src, gain in items:
            g = 1.0 if gain is None else self.col(gain, k)
            done = V.did(V.e.scalar_tensor_tensor(low[:, k, 0:width], src, g,
                                                  high[:, k, 0:width].bitcast(F32), ALU.mult, ALU.subtract))
        return done

    def norm_to_xT(self, src, tiles, width, gain, dst, ready, hn=None):
        r = self.rms_scale(src, tiles, width, ready)
        if hn is None:
            hn = self.work[:, 0:3 * D].rearrange("p (t d) -> p t d", t=3)
        for t, rows in enumerate(tiles):
            normed = self.v(lambda e: e.tensor_scalar(hn[0:rows, t, 0:width], src(t, rows), r[0:rows, t:t + 1],
                                                      None, ALU.mult))
        return self.turn(lambda t, rows, k: hn[0:rows, t, k * P:(k + 1) * P], tiles, width // P, dst,
                         normed, gain)

    def load_row(self, name, slot):
        k = WIDE_ROWS.index(name)
        return self.load(self.wide[:, slot, :], self.a["wide_rows"][:, k * D:(k + 1) * D].to_broadcast([P, D]))

    def final_norm(self, gain, ready, out=None):
        loaded = self.load_row(gain, 0)
        r = self.rms_scale(lambda t, rows: self.h[0:rows, t, :], [P] * NT, D, ready)
        for t in range(NT):
            done = self.v(lambda e: e.scalar_tensor_tensor(self.h[:, t, :], self.h[:, t, :], r[:, t:t + 1],
                                                           self.wide[:, 0, :], ALU.mult, ALU.mult), loaded)
        return done

    def split(self, at):
        flow, slot = self.c.flow, at.n % PARTS
        if type(at.turns) is int and at.n >= self.c.n_chunks:
            return
        ring, high, low = (buf[:, slot, :] for buf in (self.ring, self.high, self.low))
        for half in range(2):
            cols = slice(half * HALF, (half + 1) * HALF)
            self.A.e.wait_ge(flow.landed[slot][half], at.turns * 16 + (at.n // RING + 1) * 16)
            if half == 0 and (type(at.turns) is not int or at.n >= PARTS):
                self.A.e.wait_ge(flow.used, at.count(1 - PARTS))
            self.A.e.copy(high[:, cols], ring[:, cols]).then_inc(flow.high_made, 1)
            self.V.e.wait_ge(flow.high_made, at.halves(half + 1))
            self.V.e.tensor_tensor(low[:, cols], ring[:, cols], high[:, cols].bitcast(F32),
                                   ALU.subtract).then_inc(flow.split, 1)

    def start_split(self, first):
        for k in range(AHEAD):
            self.split(At(first + k))

    def wait_chunk(self, at):
        self.T.e.wait_ge(self.c.flow.split, at.halves(2))

    def times(self, out, x, w, start, stop, **more):
        e = self.T.e
        e.matmul(out, x[0], w[0], start=start, stop=False, **more)
        e.matmul(out, x[0], w[1], start=False, stop=False, **more)
        return e.matmul(out, x[1], w[0], start=False, stop=stop, **more)

    def weights(self, at, lo, n):
        slot = at.n % PARTS
        return self.high[:, slot, lo:lo + n], self.low[:, slot, lo:lo + n]

    def linear(self, n_chunks, tiles, evac, ready):
        c, T = self.c, self.T
        high, low = self.xT
        T.wait(ready)
        self.fence()
        if self.unsplit is not None:
            for lane in (self.T, self.A, self.V):
                lane.wait(self.all_params)
            self.start_split(self.unsplit)
            self.unsplit = None

        def one(j, at, number):
            self.split(at + AHEAD)
            self.wait_chunk(at)
            for t, rows in enumerate(tiles):
                out = self.ps[0:rows, j, t * CW:(t + 1) * CW] if t < NT else self.ps[0:rows, 3 + j, 0:CW]
                for kt in range(KT):
                    x = (high[:, kt, t * P:t * P + rows], low[:, kt, t * P:t * P + rows])
                    ins = self.times(out, x, self.weights(at, kt * CW, CW), kt == 0, kt == KT - 1)
            ins.then_inc(c.flow.used, 1)
            return evac(j, number, (c.flow.used, at.count(1)))

        c0 = c.chunk
        number, done, last = 0, None, {}
        if c0 == 0:
            for j in range(3):
                one(j, At(j), j)
            number = 3
        turns = (n_chunks - number) // 3
        if turns > 1:
            first = number
            with c.loop(turns, (T, self.A, self.V)) as (i, label, prev):
                for j in range(3):
                    T.wait(prev(f"bank{j}", self.evac_lane))
                    one(j, At(c0 + first + j, i), i * 3 + (first + j))
                    label(f"bank{j}", self.evac_lane)
            number = first + 3 * turns
            done = self.evac_lane.now()
            T.wait(done)
        for m in range(number, n_chunks):
            T.wait(last.get(m % 3))
            last[m % 3] = done = one(m % 3, At(c0 + m), m)
        c.chunk = c0 + n_chunks
        return done

    def to(self, dst, func=None):
        self.evac_lane = self.A
        A = self.A

        def evac(j, number, products, meta=True):
            A.wait(products)
            cols = ds(number * CW, CW) if type(number) is not int else slice(number * CW, (number + 1) * CW)
            got = self.ps[:, j, :].rearrange("p (t w) -> p t w", t=NT)
            if func is None:
                ins = A.e.copy(dst[:, 0:NT, cols], got)
            else:
                ins = A.e.activation(dst[:, 0:NT, cols], got, func)
            done = A.did(ins)
            if self.with_meta:
                done = A.did(A.e.copy(dst[0:META, NT, cols], self.ps[0:META, 3 + j, 0:CW]))
            return done
        return evac

    with_meta = False

    def add_to_h(self):
        self.evac_lane = self.V
        V = self.V

        def evac(j, number, products):
            V.wait(products)
            cols = ds(number * CW, CW) if type(number) is not int else slice(number * CW, (number + 1) * CW)
            got = self.ps[:, j, :].rearrange("p (t w) -> p t w", t=NT)
            return V.did(V.e.tensor_tensor(self.h[:, 0:NT, cols], self.h[:, 0:NT, cols], got, ALU.add))
        return evac

    def swiglu(self, nt, x, at, y, between=None):
        c, T, A, V, ps, w = self.c, self.T, self.A, self.V, self.ps, self.work
        n = nt * P
        act = w[:, SWI:SWI + 512].rearrange("p (f t w) -> p f t w", f=2, t=NT)
        silu = w[:, SWI + 512:SWI + 1024].rearrange("p (f t w) -> p f t w", f=2, t=NT)
        high, low = (part[:, 0:512].rearrange("p (f s) -> p f s", f=2) for part in self.smallT)
        hidden = ps[:, 4:6, :].rearrange("p f (t m w) -> p f t m w", t=NT, m=2)
        ident = self.const("ident")

        def up(f, at):
            self.split(at + AHEAD)
            self.wait_chunk(at)
            for t in range(nt):
                for kt in range(KT):
                    ins = self.times(ps[:, 4 + f, t * CW:(t + 1) * CW], x(kt, t), self.weights(at, kt * CW, CW),
                                     kt == 0, kt == KT - 1)
            ins.then_inc(c.flow.used, 1)
            return (c.flow.used, at.count(1))

        def activate(f, products, turned):
            A.wait(products, V.now())
            s = A.did(A.e.activation(silu[:, f, 0:nt, :], hidden[:, f, 0:nt, 0, :], ACT.Silu))
            V.wait(s, turned)
            return V.did(V.e.tensor_tensor(act[:, f, 0:nt, :], hidden[:, f, 0:nt, 1, :], silu[:, f, 0:nt, :],
                                           ALU.mult))

        def transpose(f, acted):
            T.wait(acted)
            for t in range(nt):
                ins = T.e.transpose(ps[:, 6 + f, t * P:(t + 1) * P], act[:, f, t, :], ident)
            turned = T.did(ins)
            A.wait(turned)
            made = A.did(A.e.copy(high[:, f, 0:n], ps[:, 6 + f, 0:n]))
            V.wait(made)
            return turned, V.did(V.e.tensor_tensor(low[:, f, 0:n], ps[:, 6 + f, 0:n],
                                                   high[:, f, 0:n].bitcast(F32), ALU.subtract))

        def down(f, parts, at):
            T.wait(parts)
            for t in range(nt):
                for half in range(2):
                    ins = self.times(y(t, half), (high[:, f, t * P:(t + 1) * P], low[:, f, t * P:(t + 1) * P]),
                                     self.weights(at, f * D + half * 512, 512), False, False,
                                     skip_group_check=True)
            return ins

        activate(0, up(0, at), None)
        if between is not None:
            between(0)
        activate(1, up(1, at + 1), None)
        with c.loop(FG - 1, (T, A, V)) as (i, label, prev):
            k = At(at.n + 2, at.turns + i)
            turned0, parts0 = transpose(0, prev("low1", V))
            activated = up(0, k)
            activate(0, activated, turned0)
            turned1, parts1 = transpose(1, prev("act1", V))
            label("low1", V)
            self.split(k + 1 + AHEAD)
            self.wait_chunk(k + 1)
            down(0, parts0, k + 1)
            down(1, parts1, k + 1).then_inc(c.flow.used, 1)
            products = up(1, k + 2)
            activate(1, products, turned1)
            label("act1", V)
        k = At(at.n + 3 * FG - 1, at.turns)
        turned0, parts0 = transpose(0, V.now())
        turned1, parts1 = transpose(1, None)
        self.split(k + AHEAD)
        if between is not None:
            between(1)
        self.wait_chunk(k)
        down(0, parts0, k)
        return down(1, parts1, k), k

    def open_banks(self, banks):
        T, V = self.T, self.V
        zero = self.small[0:1, 64:192]
        zeros = self.logit[0:1, 0, :, :].rearrange("p a b -> p (a b)")[:, 0:512]
        V.did(V.e.memset(zero, 0.0))
        T.wait(V.did(V.e.memset(zeros, 0.0)))
        self.zero, self.zeros = zero, zeros
        for b in banks:
            T.e.matmul(self.ps[:, b, :], zero, zeros, start=True, stop=False, skip_group_check=True)

    def close_banks(self, banks):
        for b in banks:
            ins = self.T.e.matmul(self.ps[:, b, :], self.zero, self.zeros, start=False, stop=True,
                                  skip_group_check=True)
        return ins

    def dense_swiglu(self, ready):
        c, T, V, ps = self.c, self.T, self.V, self.ps
        T.wait(ready)
        self.fence()
        self.open_banks(range(4))
        high, low = self.xT
        self.swiglu(NT, lambda kt, t: (high[:, kt, t * P:(t + 1) * P], low[:, kt, t * P:(t + 1) * P]),
                    At(c.chunk), lambda t, half: ps[:, 2 * t + half, :])
        self.close_banks(range(4)).then_inc(c.flow.used, 1)
        c.chunk += FFN_CHUNKS
        V.wait((c.flow.used, c.chunk))
        for t in range(NT):
            done = V.did(V.e.tensor_tensor(self.h[:, t, :], self.h[:, t, :],
                                           ps[:, 2 * t:2 * t + 2, :].rearrange("p b w -> p (b w)"), ALU.add))
        return done

    def attend(self, heads, dh, nk, q, k, values, blocks, scale, bias, out, dv, ready, sink=None,
               gate=None):
        T, A, V, ps = self.T, self.A, self.V, self.ps
        ident = self.const("ident")
        nmax = self.small[:, 64:96].rearrange("p (h t) -> p h t", t=NT)
        total = self.small[:, 96:128].rearrange("p (h t) -> p h t", t=NT)
        extra = self.small[:, 128:160].rearrange("p (h t) -> p h t", t=NT)
        whole = [b for b in range(len(blocks)) if blocks[b][1] == P]
        keys = [nk - P, nk]
        T.wait(*ready)
        self.fence()
        soft, scored, turned, spread, outed, weighed = {}, {}, {}, {}, {}, {}

        def scores(h):
            L = self.logit[:, h % 2, :, 0:nk]
            T.wait(scored.get(h - 2))
            for t in range(NT):
                ins = T.e.matmul(ps[:, 2 * (h % 2) + t, 0:keys[t]], q(h, t), k(h)[:, 0:keys[t]], start=True, stop=True)
            s = T.did(ins)
            V.wait(s, turned.get(h - 2), *ready)
            for t in range(NT):
                scored[h] = V.did(V.e.scalar_tensor_tensor(L[:, t, 0:keys[t]], ps[:, 2 * (h % 2) + t, 0:keys[t]],
                                                           scale, bias(h)[:, t, 0:keys[t]], ALU.mult, ALU.add))
            V.wait(scored[h])
            for t in range(NT):
                top = V.did(V.e.tensor_reduce(nmax[:, h, t:t + 1], L[:, t, 0:keys[t]], AX_X, ALU.max, negate=True))
            if sink is not None:
                V.wait(top)
                V.did(V.e.tensor_scalar(extra[:, h, :], nmax[:, h, :], -1.0, sink(h), ALU.mult, ALU.max))
                V.wait(V.now())
                top = V.did(V.e.tensor_scalar(nmax[:, h, :], extra[:, h, :], -1.0, None, ALU.mult))
            A.wait(top)
            for t in range(NT):
                done = A.did(A.e.activation(L[:, t, 0:keys[t]], L[:, t, 0:keys[t]], ACT.Exp, bias=nmax[:, h, t:t + 1],
                                            accum_out=total[:, h, t:t + 1]))
            if sink is not None:
                done = A.did(A.e.activation(extra[:, h, :], nmax[:, h, :], ACT.Exp, bias=sink(h)))
            soft[h] = done

        def transpose(h):
            L = self.logit[:, h % 2, :, :]
            bank = 4 + 2 * (h % 2)
            T.wait(soft[h], spread.get(h - 2), outed.get(h - 2))
            for t in range(NT):
                for n, b in enumerate(whole[:t + 1]):
                    col = blocks[b][0]
                    ins = T.e.transpose(ps[:, bank, (t * NT + n) * P:(t * NT + n + 1) * P],
                                        L[:, t, col:col + P], ident)
                for b, (col, rows) in enumerate(blocks):
                    if rows < P:
                        ins = T.e.transpose(ps[0:rows, bank + 1, t * P:(t + 1) * P],
                                            L[:, t, col:col + rows], ident)
            turned[h] = T.did(ins)
            A.wait(turned[h], weighed.get(h - 2))
            for t in range(NT):
                cols = slice(t * NT * P, (t * NT + t + 1) * P)
                done = A.did(A.e.copy(self.probT[:, h % 2, :, :].rearrange("p b w -> p (b w)")[:, cols],
                                      ps[:, bank, cols]))
            if len(blocks) > len(whole):
                done = A.did(A.e.copy(self.probM[:, h % 2, :, :].rearrange("p b w -> p (b w)"),
                                      ps[0:META, bank + 1, 0:NT * P]))
            spread[h] = done

        def weigh(h):
            bank = 5 + 2 * (h % 2)
            T.wait(spread[h])
            for t in range(NT):
                last = len(blocks) - NT + t
                for b, (col, rows) in enumerate(blocks[:last + 1]):
                    left = self.probT[:, h % 2, t * NT + whole.index(b), :] if rows == P else \
                        self.probM[:, h % 2, t, :]
                    ins = T.e.matmul(ps[:, bank, 256 + t * dv:256 + (t + 1) * dv], left, values(h, b),
                                     start=(b == 0), stop=(b == last))
            weighed[h] = T.did(ins)
            if sink is not None:
                V.wait(soft[h])
                V.did(V.e.tensor_tensor(total[:, h, :], total[:, h, :], extra[:, h, :], ALU.add))
                V.wait(V.now())
            V.wait(soft[h])
            V.did(V.e.reciprocal(total[:, h, :], total[:, h, :]))
            V.wait(V.now(), weighed[h])
            got = ps[:, bank, 256:256 + NT * dv].rearrange("p (t w) -> p t w", t=NT)
            outed[h] = V.did(V.e.tensor_tensor(out(h), got, total[:, h, :].unsqueeze(2).to_broadcast([P, NT, dv]),
                                               ALU.mult))
            if gate is not None:
                V.wait(outed[h])
                V.did(V.e.tensor_tensor(out(h), out(h), gate(h), ALU.mult))

        for s in range(heads + 2):
            if s < heads:
                scores(s)
            if 0 <= s - 1 < heads:
                transpose(s - 1)
            if s >= 2:
                weigh(s - 2)
        return self.V.now()

    def turn_heads(self, jobs, ready):
        T, A, V = self.T, self.A, self.V
        ident = self.const("ident")
        freed = [None] * 4
        T.wait(*ready, A.now(), V.now())
        for n, (sources, dst) in enumerate(jobs):
            bank = n % 4
            T.wait(freed[bank])
            at = 0
            for src, rows in sources:
                width = src.shape[-1]
                ins = T.e.transpose(self.ps[0:width, bank, at:at + rows], src, ident[0:rows, 0:rows])
                at += rows
            done = T.did(ins)
            lane = A if n % 2 else V
            lane.wait(done)
            got = self.ps[0:width, bank, 0:at]
            freed[bank] = A.did(A.e.copy(dst, got)) if lane is A else V.did(V.e.tensor_copy(dst, got))
        return A.now(), V.now()

    def product(self, k_tiles, cols, tiles, xT, evac):
        c, T = self.c, self.T
        self.fence()
        at = At(c.chunk)
        self.split(at + AHEAD)
        self.wait_chunk(at)
        for n in range(cols // CW):
            for t, rows in enumerate(tiles):
                out = self.ps[0:rows, n, t * CW:(t + 1) * CW] if t < NT else self.ps[0:rows, 4 + n, 0:CW]
                for kt in range(k_tiles):
                    x = tuple(part[:, kt, t * P:t * P + rows] for part in xT)
                    ins = self.times(out, x, self.weights(at, kt * cols + n * CW, CW), kt == 0, kt == k_tiles - 1)
            if n < cols // CW - 1:
                done = evac(n, T.did(ins))
        ins.then_inc(c.flow.used, 1)
        c.chunk += 1
        return evac(cols // CW - 1, (c.flow.used, c.chunk))

    def set_up(self):
        a = self.a
        s_first = self.c.nc.alloc_semaphore("first_landed")
        for dst, src in ((self.h[:, :, :], a["x"].rearrange("b (t p) d -> p (b t) d", p=P)),
                         (self.cols[:, :], a["cols"]), (self.consts[:, :], a["consts"])):
            self.A.e.dma_start(dst, src).then_inc(s_first, 16)
        first = (s_first, 3 * 16)
        self.c.nc.sync.wait_ge(*first)
        self.load(self.rows[:, :], a["rows"].to_broadcast([P, N_ROWS]))
        self.load(self.logit[0:33, 0].rearrange("p t k -> p (t k)")[:, 0:512], a["buckets"][:, 0:512])
        self.load(self.logit[0:33, 1].rearrange("p t k -> p (t k)")[:, 0:512], a["buckets"][:, 512:1024])
        masked = self.V.did(self.V.e.memset(self.small[0:33, 192:200], NEG))
        self.A.wait(masked)
        return first, self.load(self.small[0:32, 192:200], a["rel_bias"])

    def bias_vectors(self, ready):
        T, A = self.T, self.A
        T.wait(ready)
        for kind in range(2):
            ins = T.e.matmul(self.ps[0:8, 6 + kind, :], self.small[0:33, 192:200],
                             self.logit[0:33, kind].rearrange("p t k -> p (t k)")[:, 0:512], start=True, stop=True)
        made = T.did(ins)
        flat = self.mix[0:8, 0, 0:1024]
        copied = self.s(lambda e: e.copy(flat, self.ps[0:8, 6:8, :].rearrange("p b w -> p (b w)")), made)
        A.wait(copied)
        for kind in range(2):
            stored = self.load(self.u[kind], self.mix[0:8, 0, kind * 512:(kind + 1) * 512])
        return stored

    def load_bias(self, kind, ready):
        flat = self.logit[:, :, :, :].rearrange("p a t k -> p (a t k)")
        self.shifted = [[self.wide[:, b // 2, (b % 2) * 512:(b % 2 + 1) * 512] for b in range(4)],
                        [self.mix[:, 0, 512:1024], self.mix[:, 1, 512:1024], flat[:, 0:512], flat[:, 512:1024]]]
        self.A.wait(ready)

        def src(t, head, heads):
            return bass.AP(tensor=self.u.tensor, offset=(kind * 8 + head) * 512 + (1 - t) * P,
                           ap=[[1, P], [512, heads], [1, SEQ]])
        self.load(self.wide[:, :, :].rearrange("p a (h k) -> p (a h) k", k=SEQ), src(0, 0, 8))
        for b in range(2):
            self.load(self.shifted[1][b].rearrange("p (h k) -> p h k", k=SEQ), src(1, 2 * b, 2))
        return self.load(flat[:, 0:1024].rearrange("p (h k) -> p h k", k=SEQ), src(1, 4, 4))

    def bias_tiles(self, dst, loaded):
        T, A, V = self.T, self.A, self.V
        self.fence()
        T.wait(loaded)
        read = {}
        for n in range(2 * 4):
            t, b = n // 4, n % 4
            T.wait(read.get(n - 4))
            ins = T.e.matmul(self.ps[:, b, :], self.const("flip"), self.shifted[t][b], start=True, stop=True)
            made = T.did(ins)
            lane = A if b % 2 else V
            lane.wait(made)
            out = dst[:, t, 2 * b:2 * b + 2, :].rearrange("p h k -> p (h k)")
            read[n] = A.did(A.e.copy(out, self.ps[:, b, :])) if lane is A else \
                V.did(V.e.tensor_copy(out, self.ps[:, b, :]))

    def head_rms(self, buf, heads, gain, factor, ready):
        n = NT * heads
        view = buf.rearrange("p t (h e) -> p t h e", h=heads)
        sq = self.work[:, 4096:4096 + n * P].rearrange("p (t h e) -> p t h e", t=NT, h=heads)
        ss, r, tmp = self.small[:, 12:12 + n], self.small[:, 20:20 + n], self.small[:, 28:28 + n]
        self.v(lambda e: e.tensor_tensor(sq, view, view, ALU.mult), ready)
        self.v(lambda e: e.tensor_reduce(ss, self.work[:, 4096:4096 + n * P].rearrange("p (g e) -> p g e", e=P),
                                         AX_X, ALU.add))
        ms = self.v(lambda e: e.tensor_scalar(ss, ss, 1.0 / P, 1e-6, ALU.mult, ALU.add))
        self.rsqrt(r, ss, tmp, ms)
        rb = r.rearrange("p (t h) -> p t h", t=NT).unsqueeze(3).to_broadcast([P, NT, heads, P])
        self.v(lambda e: e.tensor_tensor(view, view, rb, ALU.mult))
        for t in range(NT):
            gb = self.row(gain).unsqueeze(1).to_broadcast([P, heads, P])
            done = self.v(lambda e: e.scalar_tensor_tensor(view[:, t], view[:, t], factor, gb, ALU.mult, ALU.mult))
        return done

    def gla(self, pr):
        T, A, V, ps, w = self.T, self.A, self.V, self.ps, self.work
        H = 4

        def area(at, *shape):
            n = 1
            for s in shape:
                n *= s
            names = "abc"[:len(shape)]
            spec = " ".join(names)
            v = w[:, at:at + n]
            return v if len(shape) == 1 else v.rearrange(f"p ({spec}) -> p {spec}", **dict(zip(names, shape)))

        qeT, keT = area(0, H, SEQ), area(1024, H, SEQ)
        kd = area(2048, NT, 256)
        g = area(2560, NT, 256)
        t1, t2, t3 = area(3072, NT, 256), area(3584, NT, 256), area(4096, NT, 256)
        qe, ke = area(4608, NT, 256), area(5120, NT, 256)
        state = area(5632, 3, H * P)
        up, downT = w[0:17, 7168:7424], w[0:17, 7424:7680]
        attT = w[:, 7680:8704].rearrange("p (h t c) -> p h t c", h=H, t=NT)
        decay = w[0:64, 8704:8720]
        self.fence()
        up_loaded = self.load(up, self.a["gla_up"])
        ones = V.did(V.e.memset(downT, 1.0))
        zeroed = V.did(V.e.memset(attT, 0.0))
        A.wait(ones)
        V.wait(ones)
        d = self.turn_heads([([(pr[:, t, 2816:2832], P) for t in range(NT)], downT[0:16, :])], ())
        T.wait(*d, up_loaded)
        for t in range(NT):
            ins = T.e.matmul(ps[:, 4, t * 256:(t + 1) * 256], downT[:, t * P:(t + 1) * P], up, start=True, stop=True)
        z_made = T.did(ins)
        z = ps[:, 4, :].rearrange("p (t w) -> p t w", t=NT)
        read = self.s(lambda e: e.activation(t1, z, ACT.Abs), z_made)
        self.v(lambda e: e.tensor_scalar(g, z, 0.0, None, ALU.min), read)
        self.s(lambda e: e.activation(t1, t1, ACT.Exp, scale=-1.0))
        logged = self.s(lambda e: e.activation(t1, t1, ACT.Ln, bias=1.0))
        self.v(lambda e: e.tensor_tensor(g, g, t1, ALU.subtract), logged)
        gated = self.v(lambda e: e.tensor_scalar(g, g, 1.0 / 16.0, None, ALU.mult))
        T.wait(gated)
        for t in range(NT):
            T.e.matmul(ps[:, 5, t * 256:(t + 1) * 256], self.const("tri"), g[:, t, :], start=True, stop=True)
            T.e.matmul(ps[:, 6, t * 256:(t + 1) * 256], self.const("same"), g[:, t, :], start=True, stop=True)
            for h in range(H):
                ins = T.e.matmul(ps[0:64, 7, (h * NT + t) * 2:(h * NT + t) * 2 + 2],
                                 g[:, t, h * 64:(h + 1) * 64], self.const("half"), start=True, stop=True)
        summed = T.did(ins)
        b = ps[:, 5, :].rearrange("p (t w) -> p t w", t=NT)
        b_last = ps[:, 6, :].rearrange("p (t w) -> p t w", t=NT)
        self.s(lambda e: e.copy(t3, b), summed)
        self.s(lambda e: e.activation(t1, b, ACT.Exp))
        self.s(lambda e: e.activation(t2, b, ACT.Exp, scale=-1.0))
        exps = self.s(lambda e: e.activation(decay, ps[0:64, 7, 0:16], ACT.Exp))
        self.v(lambda e: e.scalar_tensor_tensor(qe, pr[:, :, 0:256], 64 ** -0.5, t1, ALU.mult, ALU.mult), exps)
        self.v(lambda e: e.tensor_tensor(ke, pr[:, :, 256:512], t2, ALU.mult))
        left = self.v(lambda e: e.tensor_tensor(t3, b_last, t3, ALU.subtract))
        ends = self.s(lambda e: e.activation(t3, t3, ACT.Exp), left)
        kd_made = self.v(lambda e: e.tensor_tensor(kd, pr[:, :, 256:512], t3, ALU.mult), ends)
        jobs = []
        for src, dst in ((qe, qeT), (ke, keT)):
            for h in (0, 2):
                jobs.append(([(src[:, t, (h + u) * 64:(h + u + 1) * 64], P) for u in range(2) for t in range(NT)],
                             dst[0:64, h:h + 2, :].rearrange("p h w -> p (h w)")))
        d = self.turn_heads(jobs, (kd_made,))
        T.wait(*d)
        for h in range(H):
            for t in range(NT):
                ins = T.e.matmul(ps[:, h, t * P:(t + 1) * P], keT[0:64, h, t * P:(t + 1) * P],
                                 qeT[0:64, h, t * P:(t + 1) * P], start=True, stop=True)
        scored = T.did(ins)
        self.silu(pr[:, :, 1024:1536])
        self.silu(pr[:, :, 2304:2816])
        V.wait(scored, zeroed)
        mask = self.const("tri").bitcast(U32).unsqueeze(1).to_broadcast([P, NT, P])
        for h in range(H):
            kept = V.did(V.e.copy_predicated(attT[:, h], mask, ps[:, h, 0:256].rearrange("p (t c) -> p t c", t=NT)))
        for n in range(3):
            t, lo = n // 2, 64 * (n % 2)
            for h in range(H):
                ins = T.e.matmul(ps[0:64, 4 + n, h * P:(h + 1) * P], kd[lo:lo + 64, t, h * 64:(h + 1) * 64],
                                 pr[lo:lo + 64, t, 512 + h * P:512 + (h + 1) * P], start=True, stop=True)
        added = T.did(ins)
        self.v(lambda e: e.tensor_copy(state[0:64, 0, :], ps[0:64, 4, :]), added)
        for n in (1, 2):
            for h in range(H):
                k = (h * NT + n // 2) * 2 + n % 2
                states = self.v(lambda e: e.scalar_tensor_tensor(
                    state[0:64, n, h * P:(h + 1) * P], state[0:64, n - 1, h * P:(h + 1) * P], decay[:, k:k + 1],
                    ps[0:64, 4 + n, h * P:(h + 1) * P], ALU.mult, ALU.add))
        T.wait(kept, states)
        for h in range(H):
            for t in range(NT):
                T.e.matmul(ps[:, h, t * P:(t + 1) * P], attT[:, h, t, :], pr[:, t, 512 + h * P:512 + (h + 1) * P],
                           start=True, stop=False, skip_group_check=True)
                for half in range(2):
                    n = 2 * t + half
                    if n:
                        lo = 64 * half
                        ins = T.e.matmul(ps[lo:lo + 64, h, t * P:(t + 1) * P], qeT[0:64, h, n * 64:(n + 1) * 64],
                                         state[0:64, n - 1, h * P:(h + 1) * P], start=False, stop=(half == 1),
                                         skip_group_check=True)
        made = T.did(ins)
        out = self.mix[:, :, 0:512]
        for t in range(NT):
            copied = self.s(lambda e: e.copy(self.mix[:, t, 0:512].rearrange("p (h e) -> p h e", h=H),
                                             ps[:, 0:H, t * P:(t + 1) * P]), made)
        self.head_rms(out, H, "gla", 1.0, copied)
        return self.v(lambda e: e.tensor_tensor(out, out, pr[:, :, 1024:1536], ALU.mult), copied)

    def silu(self, x):
        return self.s(lambda e: e.activation(x, x, ACT.Silu))

    def mix_to_xT(self, ready, tiles_k=KT):
        return self.turn(lambda t, rows, k: self.mix[0:rows, t, k * P:(k + 1) * P], [P] * NT, tiles_k,
                         self.xT, ready)

    def h_tile(self, t, rows):
        return self.h[0:rows, t, :]

    def block1(self, ready):
        w, two = self.work, [P] * NT
        pr = self.proj[:, 0:2 * 3072].rearrange("p (t c) -> p t c", t=NT)
        bias = w[:, 0:4096].rearrange("p (t h k) -> p t h k", t=NT, h=8)
        qT = w[:, 4096:6144].rearrange("p (h s) -> p h s", h=8)
        kT = w[:, 6144:6656].rearrange("p (h s) -> p h s", h=2)
        normed = self.norm_to_xT(self.h_tile, two, D, "norm0", self.xT, ready)
        self.linear(N_IN1, two, self.to(pr), normed)
        stored = self.bias_vectors(self.all_params)
        loaded = self.load_bias(1, stored)
        self.gla(pr)
        self.bias_tiles(bias, loaded)
        jobs = []
        for h in range(0, 8, 2):
            jobs.append(([(pr[:, t, 1536 + (h + u) * 64:1536 + (h + u + 1) * 64], P) for u in range(2)
                          for t in range(NT)], qT[0:64, h:h + 2, :].rearrange("p h s -> p (h s)")))
        jobs.append(([(pr[:, t, 2048 + u * 64:2048 + (u + 1) * 64], P) for u in range(2) for t in range(NT)],
                     kT[0:64, :, :].rearrange("p h s -> p (h s)")))
        turned = self.turn_heads(jobs, ())
        sinks = self.row("sinks")
        self.attend(8, 64, SEQ, lambda h, t: qT[0:64, h, t * P:(t + 1) * P], lambda h: kT[0:64, h // 4, :],
                    lambda h, b: pr[:, b, 2176 + (h // 4) * 64:2176 + (h // 4 + 1) * 64],
                    [(0, P), (P, P)], 64 ** -0.5, lambda h: bias[:, :, h, :],
                    lambda h: self.mix[:, :, 512 + h * 64:512 + (h + 1) * 64], 64, turned,
                    sink=lambda h: sinks[:, h:h + 1],
                    gate=lambda h: pr[:, :, 2304 + h * 64:2304 + (h + 1) * 64])
        self.linear(N_OUT, two, self.add_to_h(), self.mix_to_xT(self.V.now()))
        self.fence()
        loaded = self.load_bias(0, self.T.now())
        normed = self.norm_to_xT(self.h_tile, two, D, "norm1", self.xT, self.V.now())
        pr = self.proj[:, 0:2 * 2560].rearrange("p (t c) -> p t c", t=NT)
        self.bias_tiles(bias, loaded)
        self.linear(N_ODD, two, self.to(pr), normed)
        self.silu(pr[:, :, 1536:2560])
        jobs = []
        for h in range(0, 8, 2):
            jobs.append(([(pr[:, t, (h + u) * P:(h + u + 1) * P], P) for u in range(2) for t in range(NT)],
                         qT[:, h:h + 2, :].rearrange("p h s -> p (h s)")))
        jobs.append(([(pr[:, t, 1024 + u * P:1024 + (u + 1) * P], P) for u in range(2) for t in range(NT)],
                     kT[:, :, :].rearrange("p h s -> p (h s)")))
        turned = self.turn_heads(jobs, ())
        self.attend(8, P, SEQ, lambda h, t: qT[:, h, t * P:(t + 1) * P], lambda h: kT[:, h // 4, :],
                    lambda h, b: pr[:, b, 1280 + (h // 4) * P:1280 + (h // 4 + 1) * P],
                    [(0, P), (P, P)], P ** -0.5, lambda h: bias[:, :, h, :],
                    lambda h: self.mix[:, :, h * P:(h + 1) * P], P, turned,
                    gate=lambda h: pr[:, :, 1536 + h * P:1536 + (h + 1) * P])
        added = self.linear(N_OUT, two, self.add_to_h(), self.mix_to_xT(self.V.now()))
        self.fence()
        return self.final_norm("final1", added)

    def angles(self, ready):
        sm = self.small
        pos_i = sm[:, 200:202].bitcast(I32)
        pos, ang = sm[:, 202:204], self.work[:, 6144:6160].rearrange("p (t f) -> p t f", t=NT)
        out = self.work[:, 6160:6192].rearrange("p (c t f) -> p c t f", c=2, t=NT)
        k = self.work[:, 6192:6208].rearrange("p (t f) -> p t f", t=NT)
        loaded = self.load(pos_i, self.a["positions"])
        self.v(lambda e: e.tensor_copy(pos, pos_i), loaded)
        for t in range(NT):
            self.v(lambda e: e.tensor_scalar(ang[:, t, :], self.row("freq"), pos[:, t:t + 1], None, ALU.mult))
        big = 12582912.0
        for c, shift in ((0, 0.25), (1, 0.0)):
            self.v(lambda e: e.tensor_scalar(k, ang, 1.0 / (2 * PI), shift, ALU.mult, ALU.add))
            self.v(lambda e: e.tensor_scalar(k, k, big, None, ALU.add))
            self.v(lambda e: e.tensor_scalar(k, k, big, None, ALU.subtract))
            o = out[:, c]
            self.v(lambda e: e.scalar_tensor_tensor(o, k, -6.28125, ang, ALU.mult, ALU.add))
            self.v(lambda e: e.scalar_tensor_tensor(o, k, -0.0019350051879882812, o, ALU.mult, ALU.add))
            self.v(lambda e: e.scalar_tensor_tensor(o, k, -3.0199159819567e-07, o, ALU.mult, ALU.add))
            self.v(lambda e: e.tensor_scalar(o, o, shift * 2 * PI, 3.1415925, ALU.add, ALU.min))
            reduced = self.v(lambda e: e.tensor_scalar(o, o, -3.1415925, None, ALU.max))
        done = self.s(lambda e: e.activation(out, out, ACT.Sin), reduced)
        return out[:, 0], out[:, 1], done

    def rope(self, x1, x2, cos, sin, shape, scratch, ready):
        n = 1
        for s in shape:
            n *= s
        rows = x1.shape[0]
        spec = "p (h f) -> p h f"
        ta, tb, tc, td = (scratch[0:rows, k * n:(k + 1) * n].rearrange(spec, f=shape[1]) for k in range(4))
        self.v(lambda e: e.tensor_tensor(ta, x1, cos, ALU.mult), ready)
        self.v(lambda e: e.tensor_tensor(tb, x2, sin, ALU.mult))
        self.v(lambda e: e.tensor_tensor(tc, x2, cos, ALU.mult))
        self.v(lambda e: e.tensor_tensor(td, x1, sin, ALU.mult))
        self.v(lambda e: e.tensor_tensor(x1, ta, tb, ALU.subtract))
        return self.v(lambda e: e.tensor_tensor(x2, tc, td, ALU.add))

    def diff_attention(self, pr):
        w, sm = self.work, self.small
        self.fence()
        cos, sin, made = self.angles(None)
        qk = pr[:, :, 0:1024].rearrange("p t (h d) -> p t h d", d=64)
        for t in range(NT):
            self.rope(qk[:, t, :, 0:8], qk[:, t, :, 8:16], cos[:, t].unsqueeze(1).to_broadcast([P, 16, 8]),
                      sin[:, t].unsqueeze(1).to_broadcast([P, 16, 8]), (16, 8), w[:, 4096:4608], made)
        self.fence()
        qT = w[:, 0:2048].rearrange("p (h s) -> p h s", h=8)
        kT = w[:, 2048:4096].rearrange("p (h s) -> p h s", h=8)
        both = w[:, 4096:6144].rearrange("p (t h c e) -> p t h c e", t=NT, h=4, c=2)
        jobs = []
        for base, dst in ((0, qT), (512, kT)):
            for h in range(0, 8, 2):
                jobs.append(([(pr[:, t, base + (h + u) * 64:base + (h + u + 1) * 64], P) for u in range(2)
                              for t in range(NT)], dst[0:64, h:h + 2, :].rearrange("p h s -> p (h s)")))
        turned = self.turn_heads(jobs, ())
        causal = self.const("causal").rearrange("p (t k) -> p t k", t=NT)
        self.attend(8, 64, SEQ, lambda h, t: qT[0:64, h, t * P:(t + 1) * P], lambda h: kT[0:64, h, :],
                    lambda h, b: pr[:, b, 1024 + (h // 2) * P:1024 + (h // 2 + 1) * P],
                    [(0, P), (P, P)], 64 ** -0.5, lambda h: causal,
                    lambda h: both[:, :, h // 2, h % 2, :], P, turned)
        lam = self.row("lambda").rearrange("p (a b d) -> p a b d", a=2, b=2)
        prod = self.logit[:, 0, 0, 0:128].rearrange("p (a d) -> p a d", a=2)
        self.fence()
        self.v(lambda e: e.tensor_tensor(prod, lam[:, :, 0, :], lam[:, :, 1, :], ALU.mult))
        dots = self.v(lambda e: e.tensor_reduce(sm[:, 204:206], prod, AX_X, ALU.add))
        exped = self.s(lambda e: e.activation(sm[:, 204:206], sm[:, 204:206], ACT.Exp), dots)
        self.v(lambda e: e.tensor_tensor(sm[:, 206:207], sm[:, 205:206], sm[:, 204:205], ALU.subtract), exped)
        self.v(lambda e: e.tensor_scalar(sm[:, 206:207], sm[:, 206:207], 0.8 - 0.6, None, ALU.subtract))
        out = self.mix[:, :, 0:512].rearrange("p t (h e) -> p t h e", h=4)
        for t in range(NT):
            self.v(lambda e: e.scalar_tensor_tensor(out[:, t], both[:, t, :, 1, :], sm[:, 206:207],
                                                    both[:, t, :, 0, :], ALU.mult, ALU.add))
        self.fence()
        return self.head_rms(self.mix[:, :, 0:512], 4, "subln", 1.0 - (0.8 - 0.6), self.V.now())

    def conv(self, pr):
        w = self.work
        self.fence()
        z = self.mix[:, :, 512:1024]
        zT = w[:, 0:4 * 258].rearrange("p (k s) -> p k s", k=4)
        bT = w[:, 1032:1032 + 1024].rearrange("p (k s) -> p k s", k=4)
        self.v(lambda e: e.memset(w[:, 0:4 * 258], 0.0))
        made = self.v(lambda e: e.tensor_tensor(z, pr[:, :, 2048:2560], pr[:, :, 2560:3072], ALU.mult))
        self.A.wait(made)
        self.turn(lambda t, rows, k: z[:, t, k * P:(k + 1) * P], [P] * NT, 4, zT[:, :, 2:258], made)
        done = self.turn(lambda t, rows, k: pr[:, t, 1536 + k * P:1536 + (k + 1) * P], [P] * NT, 4, bT,
                         self.A.now())
        self.V.wait(done)
        cT = w[:, 2056:2056 + 1024].rearrange("p (k s) -> p k s", k=4)
        for k in range(4):
            o = cT[:, k, :]
            self.v(lambda e: e.tensor_scalar(o, zT[:, k, 0:SEQ], self.col("conv", k), None, ALU.mult), done)
            self.v(lambda e: e.scalar_tensor_tensor(o, zT[:, k, 1:257], self.col("conv", 4 + k), o, ALU.mult, ALU.add))
            self.v(lambda e: e.scalar_tensor_tensor(o, zT[:, k, 2:258], self.col("conv", 8 + k), o, ALU.mult, ALU.add))
        made = self.v(lambda e: e.tensor_tensor(cT, cT, bT, ALU.mult))
        high, low = (part[:, 4:8, 0:SEQ] for part in self.xT)
        rounded = self.s(lambda e: e.copy(high, cT), made)
        return self.v(lambda e: e.tensor_tensor(low, cT, high.bitcast(F32), ALU.subtract), rounded)

    def ple(self, layer):
        V = self.V
        two = [P] * NT
        self.fence()
        p_tm = self.work[:, 7168:7680].rearrange("p (t c) -> p t c", t=NT)
        pT = tuple(part[:, 0:512].rearrange("p (k s) -> p k s", k=2) for part in self.smallT)
        p_loaded = self.load(p_tm, self.a["p_2"][layer, 0].rearrange("(t p) c -> p t c", p=P))
        normed = self.norm_to_xT(self.h_tile, two, D, f"ple{layer}", self.xT, self.V.now())
        self.turn(lambda t, rows, k: p_tm[:, t, k * P:(k + 1) * P], two, 2, pT, p_loaded)
        gate = self.proj[:, 0:2048].rearrange("p (t c) -> p t c", t=NT)
        self.linear(N_OUT, two, self.to(gate, ACT.Sigmoid), normed)
        tmp = self.work[:, 4096:6144].rearrange("p (n t w) -> p n t w", n=4, t=NT)

        def evac(n, products):
            got = self.ps[:, n, :].rearrange("p (t w) -> p t w", t=NT)
            cols = slice(n * CW, (n + 1) * CW)
            self.v(lambda e: e.tensor_tensor(tmp[:, n], got, gate[:, :, cols], ALU.mult), products)
            return self.v(lambda e: e.tensor_tensor(self.h[:, 0:NT, cols], self.h[:, 0:NT, cols], tmp[:, n], ALU.add))
        return self.product(2, D, two, pT, evac)

    def spatial(self, z):
        T, V, w = self.T, self.V, self.work
        self.fence()
        wsT = w[:, 0:1024].rearrange("p (g t) -> p g t", g=8)
        loaded = self.load(w[:, 0:1024], self.a["spatial"])
        self.load_row("lng", 0)
        gain_loaded = self.load_row("lnb", 1)
        sm = self.small
        mu, var, r, tmp = sm[:, 0:2], sm[:, 4:6], sm[:, 8:10], sm[:, 12:14]
        vv = z[:, :, D:2 * D]
        scr = w[:, 2048:4096].rearrange("p (t c) -> p t c", t=NT)
        self.v(lambda e: e.tensor_reduce(mu, vv, AX_X, ALU.add))
        self.v(lambda e: e.tensor_scalar(mu, mu, 1.0 / D, None, ALU.mult))
        self.v(lambda e: e.tensor_tensor(vv, vv, mu.unsqueeze(2).to_broadcast([P, NT, D]), ALU.subtract))
        self.v(lambda e: e.tensor_tensor(scr, vv, vv, ALU.mult))
        self.v(lambda e: e.tensor_reduce(var, scr, AX_X, ALU.add))
        ready = self.v(lambda e: e.tensor_scalar(var, var, 1.0 / D, 1e-5, ALU.mult, ALU.add))
        self.rsqrt(r, var, tmp, ready)
        for t in range(NT):
            self.v(lambda e: e.scalar_tensor_tensor(vv[:, t, :], vv[:, t, :], r[:, t:t + 1], self.wide[:, 0, :],
                                                    ALU.mult, ALU.mult), gain_loaded)
            normed = self.v(lambda e: e.tensor_tensor(vv[:, t, :], vv[:, t, :], self.wide[:, 1, :], ALU.add))
        tril = self.const("tril").unsqueeze(1).to_broadcast([P, 8, P])
        masked = self.v(lambda e: e.tensor_tensor(wsT, wsT, tril, ALU.mult), loaded)
        T.wait(masked)
        for g in range(8):
            ins = T.e.matmul(self.ps[:, g, 0:SEQ], wsT[:, g, :], vv[:, :, g * P:(g + 1) * P], start=True, stop=True)
            made = T.did(ins)
            V.wait(made)
            cols = slice(g * P, (g + 1) * P)
            done = V.did(V.e.scalar_tensor_tensor(self.mix[:, :, cols], self.ps[:, g, 0:SEQ].rearrange(
                "p (t c) -> p t c", t=NT), self.col("bs", g), z[:, :, cols], ALU.add, ALU.mult))
        return done

    def route(self, normed, hn):
        T, A, V, w = self.T, self.A, self.V, self.work
        self.fence()
        at = [MOE]

        def area(*shape):
            n = 1
            for x in shape:
                n *= x
            v = w[:, at[0]:at[0] + n]
            at[0] += n
            return v.rearrange("p (a b) -> p a b", a=shape[0]) if len(shape) == 2 else v

        rw, lg, top, idx, idf = area(KT, 8), area(NT, 8), area(NT, 8), area(NT, 8).bitcast(U32), area(NT, 8)
        gates, place, place2, chosen = area(NT, 8), area(NT, 9), area(NT, 9), area(NT, 8)
        pick, most, ones = area(NT, 8), area(2), area(P)
        more = most[:, 1:2].bitcast(I32)
        sm = self.small
        experts = self.const("experts")
        loaded = self.load(rw, self.a["router_w_2"][0].rearrange("(k p) e -> p k e", p=P))
        T.wait(loaded, normed)
        xs = w[:, SWI:SWI + 1024].rearrange("p (k s) -> p k s", k=KT)
        for t in range(NT):
            cols = slice(t * P, (t + 1) * P)
            summed = self.v(lambda e: e.tensor_tensor(xs, self.xT[0][:, :, cols].bitcast(F32),
                                                      self.xT[1][:, :, cols].bitcast(F32), ALU.add), normed, T.now())
            T.wait(summed)
            for k in range(KT):
                ins = T.e.matmul(self.ps[:, 4, t * 8:(t + 1) * 8], xs[:, k, :], rw[:, k, :],
                                 start=(k == 0), stop=(k == KT - 1))
            made = T.did(ins)
        self.v(lambda e: e.tensor_copy(lg, self.ps[:, 4, 0:16].rearrange("p (t e) -> p t e", t=NT)), made)
        for t in range(NT):
            self.v(lambda e: e.max(top[:, t, :], lg[:, t, :]))
            self.v(lambda e: e.max_index(idx[:, t, :], top[:, t, :], lg[:, t, :]))
        self.v(lambda e: e.tensor_copy(idf, idx))
        d, e1, r = sm[:, 210:212], sm[:, 212:214], sm[:, 214:216]
        diff = self.v(lambda e: e.tensor_tensor(d, top[:, :, 1], top[:, :, 0], ALU.subtract))
        ex = self.s(lambda e: e.activation(e1, d, ACT.Exp), diff)
        self.v(lambda e: e.memset(ones, 1.0))
        self.v(lambda e: e.memset(place, 0.0))
        for t in range(NT):
            self.v(lambda e: e.tensor_scalar(chosen[:, t, :], experts, idf[:, t, 0:1], None, ALU.is_equal))
            self.v(lambda e: e.scalar_tensor_tensor(chosen[:, t, :], experts, idf[:, t, 1:2], chosen[:, t, :],
                                                    ALU.is_equal, ALU.add))
        T.wait(V.now())
        T.e.matmul(self.ps[:, 5, 0:8], self.const("upto"), chosen[:, 0, :], start=True, stop=True)
        T.e.matmul(self.ps[:, 5, 8:16], self.const("upto"), chosen[:, 1, :], start=True, stop=False)
        T.e.matmul(self.ps[:, 5, 8:16], ones, chosen[:, 0, :], start=False, stop=True)
        T.e.matmul(self.ps[:, 5, 16:24], ones, chosen[:, 0, :], start=True, stop=False)
        ins = T.e.matmul(self.ps[:, 5, 16:24], ones, chosen[:, 1, :], start=False, stop=True)
        counted = T.did(ins)
        self.v(lambda e: e.tensor_scalar(r, e1, 1.0, None, ALU.add), ex)
        self.v(lambda e: e.reciprocal(r, r))
        self.v(lambda e: e.tensor_tensor(e1, e1, r, ALU.mult))
        for t in range(NT):
            self.v(lambda e: e.tensor_scalar(gates[:, t, :], experts, idf[:, t, 0:1], r[:, t:t + 1],
                                             ALU.is_equal, ALU.mult))
            self.v(lambda e: e.tensor_scalar(pick[:, t, :], experts, idf[:, t, 1:2], e1[:, t:t + 1],
                                             ALU.is_equal, ALU.mult))
            self.v(lambda e: e.tensor_tensor(gates[:, t, :], gates[:, t, :], pick[:, t, :], ALU.add))
        ranks = self.ps[:, 5, 0:16].rearrange("p (t e) -> p t e", t=NT)
        self.v(lambda e: e.tensor_tensor(place[:, :, 0:8], ranks, chosen, ALU.mult), counted)
        self.v(lambda e: e.tensor_reduce(most[:, 0:1], self.ps[:, 5, 16:24], AX_X, ALU.max))
        self.v(lambda e: e.tensor_scalar(more, most[:, 0:1], SLOTS + 0.5, None, ALU.is_gt))
        self.v(lambda e: e.tensor_scalar(place, place, 1.0, None, ALU.subtract))
        done = self.v(lambda e: e.tensor_scalar(place2, place, float(SLOTS), None, ALU.subtract))
        return gates, (place, place2), more, done

    def moe(self, hn, gates, place):
        c, T, A, V, ps, w = self.c, self.T, self.A, self.V, self.ps, self.work
        sel = w[:, 1024:1280].rearrange("p (t s) -> p t s", t=NT)
        spread = w[:, 1280:3328].rearrange("p (e s) -> p e s", e=NEXP)
        outs = self.proj[:, 0:NEXP * D]
        slots = self.const("slots")
        self.fence()

        def tokens(u):
            return tuple(part[:, :, u * SLOTS:(u + 1) * SLOTS] for part in self.xT)

        def choose(p):
            V.wait(T.now())
            for t in range(NT):
                done = V.did(V.e.tensor_scalar(sel[:, t, :], slots, p(t), None, ALU.is_equal))
            return done

        def gather(u, bank, n):
            for k in range(4 * n, 4 * n + 4):
                for t in range(NT):
                    ins = T.e.matmul(ps[:, bank, (k % 4) * P:(k % 4 + 1) * P], hn[:, t, k * P:(k + 1) * P],
                                     sel[:, t, :], start=(t == 0), stop=(t == NT - 1))
            gathered = T.did(ins)
            A.wait(gathered)
            items = [(k, ps[:, bank, (k % 4) * P:(k % 4 + 1) * P], "ffn1") for k in range(4 * n, 4 * n + 4)]
            return self.to_parts(tokens(u), items, SLOTS)

        weighted = self.proj[:, 0:NEXP * NT * P].rearrange("p (g s) -> p g s", s=P)
        for e in range(NEXP):
            for t in range(NT):
                done = V.did(V.e.tensor_scalar(weighted[:, e * NT + t, :], slots, place[:, t, e:e + 1],
                                               gates[:, t, e:e + 1], ALU.is_equal, ALU.mult))
        T.wait(done)
        for g in range(NEXP * NT):
            ins = T.e.transpose(ps[:, 4 + g // 4, (g % 4) * P:(g % 4 + 1) * P], weighted[:, g, :], self.const("ident"))
        turned = T.did(ins)
        self.s(lambda e: e.copy(w[:, 1280:3328], ps[:, 4:8, :].rearrange("p b w -> p (b w)")), turned)
        T.wait(choose(lambda t: place[:, t, 0:1]))
        gather(0, 2, 0)
        gather(0, 3, 1)
        self.fence()
        self.open_banks(())
        c0 = c.chunk
        with c.loop(NEXP // 2, (T, A, V)) as (pair, label, prev):
            for u in range(2):
                T.wait(V.now())
                emptied = A.now()
                chosen = choose(lambda t: place[:, t, ds(pair * 2 + (u + 1), 1)])
                for b in range(2):
                    T.e.matmul(ps[:, 2 * u + b, :], self.zero, self.zeros, start=True, stop=False,
                               skip_group_check=True)

                def between(n):
                    if n == 0:
                        T.wait(emptied, chosen)
                    gather(1 - u, 2 - 2 * u + n, n)
                x = tokens(u)
                ins, last = self.swiglu(1, lambda kt, t: (x[0][:, kt, :], x[1][:, kt, :]),
                                        At(c0 + u * FFN_CHUNKS, pair * (2 * FG)),
                                        lambda t, half: ps[:, 2 * u + half, :], between)
                ins.then_inc(c.flow.used, 1)
                A.wait((c.flow.used, last.count(1)))
                A.did(A.e.copy(outs[:, ds(pair * (2 * D) + u * D, D)],
                               ps[:, 2 * u:2 * u + 2, :].rearrange("p b w -> p (b w)")))
        c.chunk = c0 + NEXP * FFN_CHUNKS + AHEAD
        self.fence_steps()
        for t in range(NT):
            for half in range(2):
                for e in range(NEXP):
                    ins = T.e.matmul(ps[:, 2 * t + half, :], spread[:, e, t * P:(t + 1) * P],
                                     outs[:, e * D + half * 512:e * D + (half + 1) * 512],
                                     start=(e == 0), stop=(e == NEXP - 1))
        ins.then_inc(c.flow.used, AHEAD)
        V.wait((c.flow.used, c.chunk))
        for t in range(NT):
            done = V.did(V.e.tensor_tensor(self.h[:, t, :], self.h[:, t, :],
                                           ps[:, 2 * t:2 * t + 2, :].rearrange("p b w -> p (b w)"), ALU.add))
        return done

    def moe_again(self, hn, gates, place2, more, routed):
        c, nc = self.c, self.c.nc
        self.fence()
        c.G.e.wait_ge(*routed)
        nc.sync.wait_ge(*routed)
        nc.sync.wait_ge(c.flow.split, 2 * c.chunk)
        engines = (ENG.PE, ENG.Activation, ENG.DVE, ENG.SP)
        flag = nc.values_load(more[0:1, 0:1], engines=engines, min_val=0, max_val=1)
        main = (c.T, c.A, c.V, c.flow, c.chunk, c.n_chunks)
        with nc.If(flag > 0):
            self.T.e.wait_ge(c.flow.used, c.chunk)
            c.flow, c.chunk, c.n_chunks = self.again, 0, NEXP * FFN_CHUNKS + AHEAD
            self.T, self.A, self.V = (Lane(lane.name, lane.e, nc.alloc_semaphore(f"again_{lane.name}_steps"))
                                      for lane in main[:3])
            self.start_split(0)
            stream_part(c, self.again, self.a["stream"], self.ring, self.moe_at,
                        self.moe_at + NEXP * FFN_CHUNKS + AHEAD, self.moe_at)
            self.moe(hn, gates, place2)
            self.fence()
            nc.sync.wait_ge(c.flow.split, 2 * c.chunk)
        c.T, c.A, c.V, c.flow, c.chunk, c.n_chunks = main
        self.T, self.A, self.V = main[:3]

    def block2(self, ready):
        two = [P] * NT
        self.fence()
        normed = self.norm_to_xT(self.h_tile, two, D, "mix0", self.xT, ready)
        pr = self.proj[:, 0:2 * 3072].rearrange("p (t c) -> p t c", t=NT)
        self.linear(N_IN2, two, self.to(pr), normed)
        attended = self.diff_attention(pr)
        self.mix_to_xT(attended, 4)
        conved = self.conv(pr)
        added = self.linear(N_OUT, two, self.add_to_h(), conved)
        self.fence()
        normed = self.norm_to_xT(self.h_tile, two, D, "ffn0", self.xT, added)
        self.dense_swiglu(normed)
        self.ple(0)
        self.fence()
        normed = self.norm_to_xT(self.h_tile, two, D, "mix1", self.xT, self.V.now())
        z = self.proj[:, 0:2 * 2048].rearrange("p (t c) -> p t c", t=NT)
        self.linear(N_CIN, two, self.to(z, ACT.Gelu), normed)
        gated = self.spatial(z)
        added = self.linear(N_OUT, two, self.add_to_h(), self.mix_to_xT(gated))
        self.fence()
        hn = self.mix[:, :, :]
        normed = self.norm_to_xT(self.h_tile, two, D, "ffn1", self.xT, added, hn)
        gates, place, more, routed = self.route(normed, hn)
        self.moe(hn, gates, place[0])
        self.moe_again(hn, gates, place[1], more, routed)
        stream_part(self.c, self.c.flow, self.a["stream"], self.ring, self.c.chunk, self.c.n_chunks, 0)
        self.unsplit = self.c.chunk
        self.ple(1)
        self.fence()
        return self.final_norm("final2", self.V.now())

    def rope3(self, x, heads, half, rows, t, name, scratch):
        cos = self.const(f"cos{half}").rearrange("p (t f) -> p t f", t=NT + 1)[0:rows, t]
        sin = self.const(f"sin{half}").rearrange("p (t f) -> p t f", t=NT + 1)[0:rows, t]
        cb = cos.unsqueeze(1).to_broadcast([rows, heads, half])
        sb = sin.unsqueeze(1).to_broadcast([rows, heads, half])
        return self.rope(x[:, :, 0:half], x[:, :, half:2 * half], cb, sb, (heads, half), scratch, None)

    def key_columns(self, dst, sources):
        return ([(sources(NT)[0:META], META)] + [(sources(t), P) for t in range(NT)], dst)

    def block3(self, ready):
        T, A, V, w = self.T, self.A, self.V, self.work
        two, three = [P] * NT, [P] * NT + [META]
        self.fence()
        meta = self.proj[0:META, 0:D]
        meta_loaded = self.load(meta, self.a["meta_tokens_3"])
        self.A.wait(meta_loaded)
        self.V.wait(meta_loaded)
        normed = self.norm_to_xT(lambda t, rows: self.h[:, t, :] if t < NT else meta, three, D, "attn3",
                                 self.xT, ready)
        pr = self.proj[:, 0:3 * 2560].rearrange("p (t c) -> p t c", t=NT + 1)
        self.with_meta = True
        self.linear(N_IN3, three, self.to(pr), normed)
        self.with_meta = False
        self.fence()
        blocks = [(0, META), (META, P), (META + P, P)]
        tile_of = (NT, 0, 1)
        cqT = tuple(part[:, 0:512].rearrange("p (k s) -> p k s", k=2) for part in self.smallT)
        ckvT = tuple(part[:, 0:KEYS3].rearrange("p (k s) -> p k s", k=1) for part in self.smallT)
        kv = w[:, 0:3072].rearrange("p (t c) -> p t c", t=3)
        qT = w[:, 3072:5120].rearrange("p (h s) -> p h s", h=8)
        kT = w[:, 5120:7296].rearrange("p (h s) -> p h s", h=8)
        q = w[:, 7296:8832].rearrange("p (t c) -> p t c", t=NT)

        def to_q(n, products):
            cols = slice(n * CW, (n + 1) * CW)
            return self.s(lambda e: e.copy(q[:, :, cols], self.ps[:, n, :].rearrange("p (t w) -> p t w", t=NT)),
                          products)

        def to_kv(n, products):
            cols = slice(n * CW, (n + 1) * CW)
            self.s(lambda e: e.copy(kv[:, 0:NT, cols], self.ps[:, n, :].rearrange("p (t w) -> p t w", t=NT)),
                   products)
            return self.s(lambda e: e.copy(kv[0:META, NT, cols], self.ps[0:META, 4 + n, 0:CW]))
        self.norm_small(pr, 256, P, three, "kv3", ckvT)
        self.product(1, D, three, ckvT, to_kv)
        self.fence()
        self.norm_small(pr, 0, 256, two, "q3", cqT)
        self.product(2, 768, two, cqT, to_q)
        self.fence()
        scratch = self.mix[:, :, :].rearrange("p t d -> p (t d)")
        for t in range(NT):
            self.rope3(q[:, t, :].rearrange("p (h d) -> p h d", h=8)[:, :, 64:96], 8, 16, P, t, "q", scratch)
        for t, rows in enumerate(three):
            self.rope3(pr[0:rows, t, 384:416].unsqueeze(1), 1, 16, rows, t, "kr", scratch)
            self.rope3(pr[0:rows, t, 928:1440].rearrange("p (h d) -> p h d", h=8), 8, 32, rows, t, "ks", scratch)
            self.rope3(pr[0:rows, t, 2464:2528].unsqueeze(1), 1, 32, rows, t, "ki", scratch)
            if rows == P:
                self.rope3(pr[0:rows, t, 416:928].rearrange("p (h d) -> p h d", h=8), 8, 32, rows, t, "qs", scratch)
                self.rope3(pr[0:rows, t, 1952:2464].rearrange("p (h d) -> p h d", h=8), 8, 32, rows, t, "qi", scratch)
        self.fence()
        jobs = []
        for h in range(0, 8, 2):
            jobs.append(([(q[:, t, (h + u) * 96:(h + u + 1) * 96], P) for u in range(2) for t in range(NT)],
                         qT[0:96, h:h + 2, :].rearrange("p h s -> p (h s)")))
        for h in range(8):
            jobs.append(self.key_columns(kT[0:64, h, :], lambda t: kv[:, t, h * P:h * P + 64]))
        self.turn_heads(jobs, ())
        T.wait(A.now(), V.now())
        at = 0
        for t, rows in ((NT, META), (0, P), (1, P)):
            ins = T.e.transpose(self.ps[0:32, 4, at:at + rows], pr[0:rows, t, 384:416], self.const("ident")[0:rows, 0:rows])
            at += rows
        turned = T.did(ins)
        self.s(lambda e: e.copy(kT[64:96, :, :], self.ps[0:32, 4, 0:KEYS3].unsqueeze(1).to_broadcast([32, 8, KEYS3])),
               turned)
        causal = self.const("causal3").rearrange("p (t k) -> p t k", t=NT)
        self.attend(8, 96, KEYS3, lambda h, t: qT[0:96, h, t * P:(t + 1) * P], lambda h: kT[0:96, h, :],
                    lambda h, b: kv[0:blocks[b][1], tile_of[b], h * P + 64:(h + 1) * P],
                    blocks, 96 ** -0.5, lambda h: causal, lambda h: self.mix[:, :, h * 64:(h + 1) * 64], 64,
                    (A.now(), V.now()))
        self.fence()
        kiT = w[:, 0:KEYS3]
        score = w[:, 272:816].rearrange("p (t k) -> p t k", t=NT)
        keep = w[:, 816:1360].rearrange("p (t k) -> p t k", t=NT)
        relu = w[:, 1360:1904].rearrange("p (t k) -> p t k", t=NT)
        qiT = w[:, 1904:3952].rearrange("p (h s) -> p h s", h=8)
        qsT = w[:, 3952:6000].rearrange("p (h s) -> p h s", h=8)
        ksT = w[:, 6000:8176].rearrange("p (h s) -> p h s", h=8)
        jobs = [self.key_columns(kiT[0:64, :], lambda t: pr[:, t, 2464:2528])]
        for base, dst in ((1952, qiT), (416, qsT)):
            for h in range(0, 8, 2):
                jobs.append(([(pr[:, t, base + (h + u) * 64:base + (h + u + 1) * 64], P) for u in range(2)
                              for t in range(NT)], dst[0:64, h:h + 2, :].rearrange("p h s -> p (h s)")))
        for h in range(8):
            jobs.append(self.key_columns(ksT[0:64, h, :], lambda t: pr[:, t, 928 + h * 64:928 + (h + 1) * 64]))
        self.turn_heads(jobs, ())
        self.index_scores(pr, qiT, kiT, score, relu)
        self.choose(score, relu, keep, causal)
        self.attend(8, 64, KEYS3, lambda h, t: qsT[0:64, h, t * P:(t + 1) * P], lambda h: ksT[0:64, h, :],
                    lambda h, b: pr[0:blocks[b][1], tile_of[b], 1440 + h * 64:1440 + (h + 1) * 64],
                    blocks, 64 ** -0.5, lambda h: keep, lambda h: self.mix[:, :, 512 + h * 64:512 + (h + 1) * 64], 64,
                    (A.now(), V.now()))
        self.fence()
        added = self.linear(N_OUT, two, self.add_to_h(), self.mix_to_xT(self.V.now()))
        self.fence()
        normed = self.norm_to_xT(self.h_tile, two, D, "ffn3", self.xT, added)
        self.dense_swiglu(normed)
        self.fence()
        return self.final_norm("final3", self.V.now())

    def norm_small(self, pr, lo, width, tiles, gain, dst):
        r = self.rms_scale(lambda t, rows: pr[0:rows, t, lo:lo + width], tiles, width, None)
        hn = self.mix[:, :, :].rearrange("p t d -> p (t d)")[:, 0:768].rearrange("p (t c) -> p t c", t=3)
        for t, rows in enumerate(tiles):
            normed = self.v(lambda e: e.tensor_scalar(hn[0:rows, t, 0:width], pr[0:rows, t, lo:lo + width],
                                                      r[0:rows, t:t + 1], None, ALU.mult))
        self.turn(lambda t, rows, k: hn[0:rows, t, k * P:(k + 1) * P], tiles, width // P, dst, normed, gain)
        self.fence()

    def index_scores(self, pr, qiT, kiT, score, relu):
        T, A, V, ps = self.T, self.A, self.V, self.ps
        self.fence()
        wi = self.small[:, 64:80].rearrange("p (t h) -> p t h", t=NT)
        self.v(lambda e: e.tensor_scalar(wi, pr[:, 0:NT, 2528:2536], 8 ** -0.5, None, ALU.mult))
        self.v(lambda e: e.memset(score, 0.0))
        for h in range(8):
            T.wait(A.now())
            for t in range(NT):
                ins = T.e.matmul(ps[:, 2 * (h % 2) + t, 0:KEYS3], qiT[0:64, h, t * P:(t + 1) * P], kiT[0:64, :],
                                 start=True, stop=True)
            made = T.did(ins)
            pos = self.s(lambda e: e.activation(relu, ps[:, 2 * (h % 2):2 * (h % 2) + 2, 0:KEYS3], ACT.Relu,
                                                scale=64 ** -0.5), made, V.now())
            for t in range(NT):
                self.v(lambda e: e.scalar_tensor_tensor(score[:, t, :], relu[:, t, :], wi[:, t, h:h + 1],
                                                        score[:, t, :], ALU.mult, ALU.add), pos)

    def choose(self, score, left, keep, causal):
        best = self.small[:, 80:96].rearrange("p (t e) -> p t e", t=NT)
        self.v(lambda e: e.tensor_tensor(left, score, causal, ALU.add))
        for _ in range(TOPK3 // 8):
            for t in range(NT):
                self.v(lambda e: e.max(best[:, t, :], left[:, t, :]))
                self.v(lambda e: e.match_replace(left[:, t, :], best[:, t, :], left[:, t, :], TAKEN))
        self.v(lambda e: e.tensor_scalar(keep, left, TAKEN, None, ALU.is_equal))
        self.v(lambda e: e.tensor_scalar(keep, keep, -NEG, NEG, ALU.mult, ALU.add))
        self.v(lambda e: e.tensor_tensor(keep, keep, causal, ALU.add))
        self.fence()


def three_blocks(nc, args, out, plan, blocks=(1, 2, 3)):
    c = Core(nc, plan)
    m = Model(c, args)
    m.u = nc.dram_tensor("bias_vectors", [2, 8, 512], F32).ap()
    c.n_chunks = args["stream"].shape[0]
    m.moe_at = (N_IN1 + 2 * N_OUT + N_ODD) * (1 in blocks) + N_IN2 + FFN_CHUNKS + 3 * N_OUT + 1 + N_CIN
    part = m.moe_at + NEXP * FFN_CHUNKS + AHEAD if 2 in blocks else c.n_chunks
    m.again = Flow(nc, "again_chunk")
    ready, m.all_params = m.set_up()
    stream_part(c, c.flow, args["stream"], m.ring, 0, part, 0)
    for lane in (c.T, c.A, c.V):
        lane.wait(ready)
    if 1 in blocks:
        ready = m.block1(ready)
    if 2 in blocks:
        ready = m.block2(ready)
    if 3 in blocks:
        ready = m.block3(ready)
    c.A.wait(ready)
    s_out = nc.alloc_semaphore("out_stored")
    c.A.e.dma_start(out.rearrange("b (t p) d -> p (b t) d", p=P), m.h[:, 0:NT, :]).then_inc(s_out, 16)
    c.A.e.wait_ge(s_out, 16)
    assert c.chunk + AHEAD - 1 == c.n_chunks, (c.chunk, c.n_chunks)



def shape_constants():
    import math
    import numpy as np
    i = np.arange(P)
    k = np.zeros((P, N_CONST), np.float32)

    def put(name, value):
        at, width = CONSTS[name]
        k[:, at:at + width] = value.reshape(P, width)

    put("ident", np.eye(P))
    put("flip", np.eye(P)[::-1])
    same = i[:, None] // 64 == i[None, :] // 64
    put("tri", same & (i[:, None] <= i[None, :]))
    put("same", same)
    put("half", i[:, None] // 64 == np.arange(2)[None, :])
    put("tril", i[:, None] <= i[None, :])
    q = i[:, None, None] + P * np.arange(NT)[None, :, None]
    put("causal", np.where(np.arange(SEQ)[None, None, :] <= q, 0.0, NEG))
    put("causal3", np.where(np.arange(KEYS3)[None, None, :] <= q + META, 0.0, NEG))
    pos = np.concatenate([META + np.arange(SEQ), np.arange(P)]).astype(np.float32).reshape(NT + 1, P).T
    for half in (16, 32):
        inv = np.power(np.float32(10000.0), -np.arange(half, dtype=np.float32) / np.float32(half))
        ang = (pos[:, :, None] * inv[None, None, :]).astype(np.float64)
        put(f"cos{half}", np.cos(ang))
        put(f"sin{half}", np.sin(ang))
    put("upto", i[:, None] <= i[None, :])
    put("slots", np.broadcast_to(np.arange(SLOTS), (P, SLOTS)))
    put("experts", np.broadcast_to(np.arange(NEXP), (P, NEXP)))
    m = np.arange(512)
    dist = 255 - m
    n = np.maximum(dist, 0)
    large = 16 + (np.log(np.maximum(n, 1).astype(np.float32) / 16) / math.log(8) * 16).astype(np.int32)
    bucket = np.where(n < 16, n, np.minimum(large, 31))
    hot = np.zeros((33, 2, 512), np.float32)
    for kind, window in enumerate((256, 128)):
        seen = (dist >= 0) & (dist < window)
        hot[bucket[seen], kind, m[seen]] = 1.0
        hot[32, kind, ~seen] = 1.0
    return k, hot.reshape(33, 1024)


def weight_stream(w):
    import numpy as np

    def wide(a):
        n = -(-a.shape[1] // CW)
        full = np.zeros((D, n * CW), a.dtype)
        full[:, :a.shape[1]] = a
        return full.reshape(KT, P, n, CW).transpose(2, 1, 0, 3).reshape(n, P, CHUNK)

    def tall(a):
        k = a.shape[0] // P
        full = np.zeros((P, CHUNK), a.dtype)
        full[:, :k * a.shape[1]] = a.reshape(k, P, -1).transpose(1, 0, 2).reshape(P, -1)
        return full[None]

    def swiglu(w1, w3, w2):
        e = w1.shape[0]
        up = np.empty((e, FF // P, P, KT, 2, P), w1.dtype)
        up[:, :, :, :, 0] = w1.reshape(e, KT, P, FF // P, P).transpose(0, 3, 2, 1, 4)
        up[:, :, :, :, 1] = w3.reshape(e, KT, P, FF // P, P).transpose(0, 3, 2, 1, 4)
        up = up.reshape(e * FG, 2, P, CHUNK)
        down = w2.reshape(e * FG, 2, P, D).transpose(0, 2, 1, 3).reshape(e * FG, P, CHUNK)
        up, down = up.reshape(e, FG, 2, P, CHUNK), down.reshape(e, FG, P, CHUNK)
        full = np.empty((e, 3 * FG, P, CHUNK), w1.dtype)
        full[:, 0:2] = up[:, 0]
        full[:, 2:-1:3] = up[:, 1:, 0]
        full[:, 3:-1:3] = down[:, :-1]
        full[:, 4:-1:3] = up[:, 1:, 1]
        full[:, -1] = down[:, -1]
        return full.reshape(-1, P, CHUNK)

    e = w["w_in_even"][0]
    e = np.concatenate([e[:, 0:1024], e[:, 1040:2832], e[:, 1024:1040]], axis=1)
    parts = [
        wide(e), wide(w["w_out_even"][0]), wide(w["w_in_odd"][0]), wide(w["w_out_odd"][0]),
        wide(w["a_w_in_2"][0]), wide(w["a_w_out_2"][0]), swiglu(w["ffn_w1_2"], w["ffn_w3_2"], w["ffn_w2_2"]),
        wide(w["ple_gate_2"][0]), tall(w["ple_proj_2"][0]), wide(w["c_w_in_2"][0]), wide(w["c_w_out_2"][0]),
        swiglu(w["moe_w1_2"][0], w["moe_w3_2"][0], w["moe_w2_2"][0]), np.zeros((AHEAD, P, CHUNK), np.float32),
        wide(w["ple_gate_2"][1]), tall(w["ple_proj_2"][1]),
        wide(w["w_in_3"][0]), tall(w["w_ukv_3"][0]), tall(w["w_uq_3"][0]), wide(w["w_o_3"][0]),
        swiglu(w["w_gate_3"], w["w_up_3"], w["w_down_3"]),
    ]
    cuts = (0, 4, 15, len(parts))
    return parts, cuts


def small_arrays(w):
    import numpy as np
    cols = np.zeros((P, N_COLS), np.float32)

    def put(name, a, width):
        at = COLS[name][0]
        cols[:, at:at + width] = a.reshape(width, P).T

    for name, a in (("norm0", w["norm_gain"][0]), ("norm1", w["norm_gain"][1]), ("mix0", w["ln_mix_2"][0]),
                    ("mix1", w["ln_mix_2"][1]), ("ffn0", w["ln_ffn_2"][0]), ("ffn1", w["ln_ffn_2"][1]),
                    ("ple0", w["ln_ple_2"][0]), ("ple1", w["ln_ple_2"][1]), ("attn3", w["attn_norm_g_3"][0]),
                    ("ffn3", w["ffn_norm_g_3"][0]), ("q3", w["mla_q_norm_g_3"][0]),
                    ("kv3", w["mla_kv_norm_g_3"][0]), ("bs", w["c_b_s_2"][0]),
                    ("conv", np.ascontiguousarray(w["a_conv_w_2"][0].T))):
        put(name, a, COLS[name][1])
    freq = np.float32(500000.0) ** (-np.arange(0, 16, 2, dtype=np.float32) / np.float32(16))
    wide_rows = np.concatenate([w["final_gain"], w["c_ln_g_2"][0], w["c_ln_b_2"][0], w["final_norm_2"],
                                w["final_norm_g_3"]])[None]
    rows = np.concatenate([w["gla_norm_gain"][0], w["a_subln_2"][0], w["swa_sinks"][0],
                           w["a_lambda_2"][0].reshape(-1), freq.astype(np.float32)])[None]
    up = np.concatenate([w["gla_w_up"][0], w["gla_b_up"][0][None]], axis=0)
    spatial = w["c_w_s_2"][0].transpose(2, 0, 1).reshape(P, 8 * P)
    return {"cols": cols, "rows": rows, "wide_rows": wide_rows, "gla_up": up, "spatial": spatial}


def build(nc_of, arrays, blocks=(1, 2, 3)):
    plan = {}
    for _ in range(2):
        nc = nc_of()
        args = {name: nc.dram_tensor(f"in_{name}", a.shape, mybir.dt.from_np(a.dtype), kind="ExternalInput").ap()
                for name, a in arrays.items()}
        out = nc.dram_tensor("out_0", (1, SEQ, D), F32, kind="ExternalOutput").ap()
        three_blocks(nc, args, out, plan, blocks)
    return nc


def host_arrays(inputs, blocks=(1, 2, 3)):
    import numpy as np
    w = {name: np.asarray(a) for name, a in inputs.items()}
    parts, cuts = weight_stream(w)
    parts = [p for b in blocks for p in parts[cuts[b - 1]:cuts[b]]]
    parts.append(np.zeros((AHEAD - 1, P, CHUNK), np.float32))
    consts, buckets = shape_constants()
    arrays = {"stream": np.concatenate(parts), "consts": consts, "buckets": buckets, **small_arrays(w)}
    arrays["positions"] = w["positions_2"].reshape(NT, P).T
    for name in ("x", "rel_bias", "p_2", "router_w_2", "meta_tokens_3"):
        arrays[name] = np.ascontiguousarray(w[name])
    return {name: np.ascontiguousarray(a) for name, a in arrays.items()}


def kernel(**inputs):
    import concourse.bacc as bacc
    from concourse.bass_utils import run_bass_kernel_spmd

    arrays = host_arrays(inputs)
    nc = build(lambda: bacc.Bacc("TRN2", target_bir_lowering=False, num_devices=1), arrays)
    result = run_bass_kernel_spmd(nc, [{f"in_{name}": a for name, a in arrays.items()}], core_ids=[0])
    return result.results[0]["out_0"]
```
